# Optimizing a Trainium2 kernel written in Bass

```python
import math
import jax, jax.numpy as jnp
from jax import lax
import numpy as np

D_MODEL = 1024
BATCH = 1
SEQ = 512
DEPTH = 1

D_FF = 2816
FOX_HEADS = 8
FOX_HEAD_DIM = 64
FOX_WIDTH = FOX_HEADS * FOX_HEAD_DIM
Q_BLOCK = 128
GLA_HEADS = 4
GLA_DK = 64
GLA_DV = 128
GLA_KEY_WIDTH = GLA_HEADS * GLA_DK
GLA_VAL_WIDTH = GLA_HEADS * GLA_DV
GLA_GATE_RANK = 16
GLA_TAU = 16.0
GLA_CHUNK = 64
NORM_EPS = 1e-6

IN_SPLITS = [FOX_WIDTH, FOX_WIDTH, FOX_WIDTH, FOX_HEADS,
             GLA_KEY_WIDTH, GLA_KEY_WIDTH, GLA_VAL_WIDTH, GLA_GATE_RANK, GLA_VAL_WIDTH,
             D_MODEL, D_MODEL]
D_IN = sum(IN_SPLITS)
IN_OFFSETS = [sum(IN_SPLITS[:i + 1]) for i in range(len(IN_SPLITS) - 1)]

kernel_name = "hybrid_fox_gla_gated_macaron"

def rmsnorm(x, g):
    xf = x.astype(jnp.float32)
    y = xf * lax.rsqrt(jnp.mean(xf * xf, axis=-1, keepdims=True) + NORM_EPS)
    return (y * g.astype(jnp.float32)).astype(x.dtype)

def swiglu(x, w_gate, w_up, w_down):
    return (jax.nn.silu(x @ w_gate) * (x @ w_up)) @ w_down

def forgetting_attention(q, k, v, log_f):
    B, S, H, Dh = q.shape
    c = jnp.cumsum(log_f, axis=1).transpose(0, 2, 1)
    scale = Dh ** -0.5
    qf, kf = q.astype(jnp.float32), k.astype(jnp.float32)
    outs = []
    for i in range(S // Q_BLOCK):
        q0 = i * Q_BLOCK
        kend = q0 + Q_BLOCK
        s = jnp.einsum('bqhd,bkhd->bhqk', qf[:, q0:kend], kf[:, :kend]) * scale
        bias = c[:, :, q0:kend, None] - c[:, :, None, :kend]
        mask = (q0 + jnp.arange(Q_BLOCK))[:, None] >= jnp.arange(kend)[None, :]
        s = jnp.where(mask, s + bias, -jnp.inf)
        p = jax.nn.softmax(s, axis=-1)
        outs.append(jnp.einsum('bhqk,bkhd->bqhd', p.astype(v.dtype), v[:, :kend]))
    return jnp.concatenate(outs, axis=1)

def gla_chunked(q, k, v, log_a):
    B, S, H, Dk = q.shape
    Dv = v.shape[-1]
    N, C = S // GLA_CHUNK, GLA_CHUNK

    def to_chunks(t):
        return t.astype(jnp.float32).reshape(B, N, C, H, t.shape[-1]).transpose(0, 3, 1, 2, 4)

    qc = to_chunks(q) * (Dk ** -0.5)
    kc, vc, gc = to_chunks(k), to_chunks(v), to_chunks(log_a)
    b = jnp.cumsum(gc, axis=3)
    b_last = b[:, :, :, -1:, :]
    q_in = qc * jnp.exp(b)
    k_in = kc * jnp.exp(-b)
    k_st = kc * jnp.exp(b_last - b)
    tril = jnp.tril(jnp.ones((C, C), dtype=bool))
    attn = jnp.where(tril, jnp.einsum('bhncd,bhnsd->bhncs', q_in, k_in), 0.0)
    o_intra = jnp.einsum('bhncs,bhnsv->bhncv', attn, vc)
    kv = jnp.einsum('bhnsd,bhnsv->bhndv', k_st, vc)
    decay = jnp.exp(b_last[:, :, :, 0, :])

    def step(state, inp):
        d, kvn = inp
        return d[..., None] * state + kvn, state

    s0 = jnp.zeros((B, H, Dk, Dv), jnp.float32)
    _, s_prev = lax.scan(step, s0, (jnp.moveaxis(decay, 2, 0), jnp.moveaxis(kv, 2, 0)))
    s_prev = jnp.moveaxis(s_prev, 0, 2)
    o = o_intra + jnp.einsum('bhncd,bhndv->bhncv', q_in, s_prev)
    return o.transpose(0, 2, 3, 1, 4).reshape(B, S, H, Dv).astype(v.dtype)

def hybrid_mixer(u, w_in, b_forget, w_alpha_up, b_alpha, gla_norm_g,
                 w_branch_fox, w_branch_gla, w_out):
    B, S, _ = u.shape
    z = u @ w_in
    (fq, fk, fv, f_logit, gq, gk, gv, a_lr, g_r, gate_fox, gate_gla) = jnp.split(z, IN_OFFSETS, axis=-1)
    log_f = jax.nn.log_sigmoid((f_logit + b_forget).astype(jnp.float32))
    o_fox = forgetting_attention(fq.reshape(B, S, FOX_HEADS, FOX_HEAD_DIM),
                                 fk.reshape(B, S, FOX_HEADS, FOX_HEAD_DIM),
                                 fv.reshape(B, S, FOX_HEADS, FOX_HEAD_DIM), log_f)
    o_fox = o_fox.reshape(B, S, FOX_WIDTH)
    log_a = jax.nn.log_sigmoid((a_lr @ w_alpha_up + b_alpha).astype(jnp.float32)) / GLA_TAU
    o_gla = gla_chunked(gq.reshape(B, S, GLA_HEADS, GLA_DK),
                        gk.reshape(B, S, GLA_HEADS, GLA_DK),
                        gv.reshape(B, S, GLA_HEADS, GLA_DV),
                        log_a.reshape(B, S, GLA_HEADS, GLA_DK))
    o_gla = rmsnorm(o_gla, gla_norm_g.reshape(GLA_HEADS, GLA_DV)).reshape(B, S, GLA_VAL_WIDTH)
    o_gla = o_gla * jax.nn.silu(g_r)
    y = jax.nn.sigmoid(gate_fox) * (o_fox @ w_branch_fox) + jax.nn.sigmoid(gate_gla) * (o_gla @ w_branch_gla)
    return y @ w_out

def setup_inputs(seed: int = 0) -> dict:
    key = jax.random.key(seed)
    ks = jax.random.split(key, 24)
    L = DEPTH

    def w(k, shape, fan_in):
        return jax.random.normal(k, shape, jnp.float32) * fan_in ** -0.5

    def gain(k, n):
        return 1.0 + 0.05 * jax.random.normal(k, (L, n), jnp.float32)

    return {
        "x": jax.random.normal(ks[0], (BATCH, SEQ, D_MODEL), jnp.float32),
        "ffn1_pre_g": gain(ks[1], D_MODEL),
        "ffn1_w_gate": w(ks[2], (L, D_MODEL, D_FF), D_MODEL),
        "ffn1_w_up": w(ks[3], (L, D_MODEL, D_FF), D_MODEL),
        "ffn1_w_down": w(ks[4], (L, D_FF, D_MODEL), D_FF),
        "ffn1_post_g": gain(ks[5], D_MODEL),
        "mix_pre_g": gain(ks[6], D_MODEL),
        "w_in": w(ks[7], (L, D_MODEL, D_IN), D_MODEL),
        "b_forget": 0.1 * jax.random.normal(ks[8], (L, FOX_HEADS), jnp.float32),
        "w_alpha_up": w(ks[9], (L, GLA_GATE_RANK, GLA_KEY_WIDTH), GLA_GATE_RANK),
        "b_alpha": 0.1 * jax.random.normal(ks[10], (L, GLA_KEY_WIDTH), jnp.float32),
        "gla_norm_g": gain(ks[11], GLA_VAL_WIDTH),
        "w_branch_fox": w(ks[12], (L, FOX_WIDTH, D_MODEL), FOX_WIDTH),
        "w_branch_gla": w(ks[13], (L, GLA_VAL_WIDTH, D_MODEL), GLA_VAL_WIDTH),
        "w_out": w(ks[14], (L, D_MODEL, D_MODEL), D_MODEL),
        "mix_post_g": gain(ks[15], D_MODEL),
        "ffn2_pre_g": gain(ks[16], D_MODEL),
        "ffn2_w_gate": w(ks[17], (L, D_MODEL, D_FF), D_MODEL),
        "ffn2_w_up": w(ks[18], (L, D_MODEL, D_FF), D_MODEL),
        "ffn2_w_down": w(ks[19], (L, D_FF, D_MODEL), D_FF),
        "ffn2_post_g": gain(ks[20], D_MODEL),
    }

def reference(x, ffn1_pre_g, ffn1_w_gate, ffn1_w_up, ffn1_w_down, ffn1_post_g,
              mix_pre_g, w_in, b_forget, w_alpha_up, b_alpha, gla_norm_g,
              w_branch_fox, w_branch_gla, w_out, mix_post_g,
              ffn2_pre_g, ffn2_w_gate, ffn2_w_up, ffn2_w_down, ffn2_post_g):
    h = x
    for l in range(DEPTH):
        f1 = swiglu(rmsnorm(h, ffn1_pre_g[l]), ffn1_w_gate[l], ffn1_w_up[l], ffn1_w_down[l])
        h = h + 0.5 * rmsnorm(f1, ffn1_post_g[l])
        m = hybrid_mixer(rmsnorm(h, mix_pre_g[l]), w_in[l], b_forget[l], w_alpha_up[l],
                         b_alpha[l], gla_norm_g[l], w_branch_fox[l], w_branch_gla[l], w_out[l])
        h = h + rmsnorm(m, mix_post_g[l])
        f2 = swiglu(rmsnorm(h, ffn2_pre_g[l]), ffn2_w_gate[l], ffn2_w_up[l], ffn2_w_down[l])
        h = h + 0.5 * rmsnorm(f2, ffn2_post_g[l])
    return h


_drawn_inputs = setup_inputs


def setup_inputs(seed=0):
    import zlib

    import numpy as np

    out = dict(_drawn_inputs(seed))
    spreads = {}
    factors = {'ffn2_post_g': 3.743}
    for name, (base, spread) in spreads.items():
        noise = np.random.default_rng([zlib.crc32(name.encode()), seed]).standard_normal(out[name].shape)
        drawn = base * np.exp(spread * noise) if base else spread * noise
        out[name] = __import__('jax').numpy.asarray(drawn.astype(out[name].dtype))
    for name, factor in factors.items():
        out[name] = (out[name] * factor).astype(out[name].dtype)
    return out
```

```python
from contextlib import ExitStack

import concourse.bass as bass
from concourse import mybir

F32 = mybir.dt.float32
F32R = mybir.dt.float32r
ACT = mybir.ActivationFunctionType
ALU = mybir.AluOpType
AX = mybir.AxisListType

P = 128
N = 512
D = 1024
FF = 2816
KD, KF, TT = D // P, FF // P, N // P
HALF = D // 2
UNIT = 1024
SLOTS = 4
EPS = 1e-6

FOX_H, FOX_D = 8, 64
GLA_H, GLA_DK, GLA_DV, CHUNK = 4, 64, 128, 64
RANK, TAU = 16, 16.0
NCH = N // CHUNK
widths = [FOX_H * FOX_D] * 3 + [FOX_H, GLA_H * GLA_DK, GLA_H * GLA_DK, GLA_H * GLA_DV, RANK, GLA_H * GLA_DV, D, D]
(C_FQ, C_FK, C_FV, C_FL, C_GQ, C_GK, C_GV, C_AL, C_GR, C_GF, C_GG) = [sum(widths[:i]) for i in range(11)]
SMALL = 48
ALR = 32

FFN_UNITS = 2 * KF + KF
U_FFN1 = 0
U_MIX = U_FFN1 + FFN_UNITS
(U_SMALL, U_FK, U_FQ, U_FV, U_GQ, U_GK, U_GV, U_GR, U_GATE, U_OUT, U_FFN2) = [
    U_MIX + x for x in (0, 1, 5, 9, 13, 15, 17, 21, 25, 49, 57)]
U_END = U_FFN2 + FFN_UNITS

CROWS = 96 + FOX_H
MASKED = -1e30
T_Q, T_K, T_V, T_GV, T_GQ, T_GK, T_KST = 0, 4, 8, 12, 16, 18, 20
T_OG = (T_GK, T_GQ, T_GK + 1, T_GQ + 1)


def slot(u):
    return u % SLOTS


def arrivals(u):
    return 16 * (u // SLOTS + 1)


A_FFN1, A_OUT, A_FFN2 = 0, KF, KF + KD
PAIRS = 2


def macaron_layer(nc, x, g1pre, w1g, w1u, w1d, g1post, gmpre, w_in, b_forget, w_alpha, b_alpha,
                  gla_g, w_bf, w_bg, w_out, gmpost, g2pre, w2g, w2u, w2d, g2post, out):
    with ExitStack() as ctx:
        def sb(name, shape, dt=F32):
            return ctx.enter_context(nc.sbuf_tensor(name, shape, dt))

        def sem(name):
            return ctx.enter_context(nc.semaphore(name))

        raw = sb("raw", [P, SLOTS, UNIT])
        w_hi = sb("w_hi", [P, SLOTS, UNIT], F32R)
        w_lo = sb("w_lo", [P, SLOTS, UNIT], F32R)
        a_hi = sb("a_hi", [P, SLOTS, N], F32R)
        a_lo = sb("a_lo", [P, SLOTS, N], F32R)
        h = sb("h", [P, TT, D])
        u_hi = sb("u_hi", [P, KD, N], F32R)
        u_lo = sb("u_lo", [P, KD, N], F32R)
        arena = sb("arena", [P, KF, N])
        og_hi = sb("og_hi", [P, GLA_H, N], F32R)
        og_lo = sb("og_lo", [P, GLA_H, N], F32R)
        of_hi, of_lo = a_hi, a_lo
        scr = sb("scr", [P, 7 * 1024])
        silu = scr[:, 0:1024].rearrange("p (b n) -> p b n", b=2)
        scaled = scr[:, 1024:2048]
        junk = scr[:, 2048:3072]
        normed = scr[:, 3072:5120].rearrange("p (b n) -> p b n", b=2)
        g_pre = scr[:, 5120:6144]
        g_post = scr[:, 6144:7168]
        probs = scr[:, 0:1024].rearrange("p (b n) -> p b n", b=2)
        probsT = scr[:, 1024:2048].rearrange("p (b n) -> p b n", b=2)
        intra = scr[:, 2048:3072].rearrange("p (b t c) -> p b t c", b=2, t=TT)
        state = scr[:, 3072:4096].rearrange("p (n v) -> p n v", n=NCH)
        ga = scr[:, 4096:5120].rearrange("p (j n) -> p j n", j=2)
        gb = scr[:, 5120:6144].rearrange("p (j n) -> p j n", j=2)
        small = scr[:, 6144:6656]
        fsum = scr[:, 6656:7168]
        w_al = scr[:, 6656:6656 + 2 * P]
        sq, rstd_g = ga, gb
        sig = scr[:, 0:2048].rearrange("p (b n) -> p b n", b=4)
        part = scr[:, 2048:4096].rearrange("p (b n) -> p b n", b=4)
        kst_tok = arena[:, T_KST:T_KST + 2, :].rearrange("p a n -> p (a n)").rearrange("p (t f) -> p t f", t=TT)

        c_parts = sb("c_parts", [CROWS, N], F32R)
        c_neg = sb("c_neg", [CROWS, N], F32R)
        head_sel = sb("head_sel", [CROWS, FOX_H, 2], F32R)
        ident_r = sb("ident_r", [P, P], F32R)
        causal = sb("causal", [P, P], F32R)
        ident = sb("ident", [P, P])
        mean_g = sb("mean_g", [P, P])
        ones = sb("ones", [P, 1])
        half_neg = sb("half_neg", [P, 1])
        eps_t = sb("eps_t", [P, 1])
        bias_small = sb("bias_small", [SMALL, 1])
        bias_alpha = sb("bias_alpha", [P, 2])
        gn = sb("gn", [P, GLA_H])
        ms_post = sb("ms_post", [P, 12])
        ms_pre = sb("ms_pre", [P, 12])
        ve_post = sb("ve_post", [P, 12])
        ve_pre = sb("ve_pre", [P, 12])
        rstd_post = sb("rstd_post", [P, 12])
        rstd_pre = sb("rstd_pre", [P, 12])
        neg_max = sb("neg_max", [P, 32])
        rowsum = sb("rowsum", [P, 32])
        rinv = sb("rinv", [P, 32])
        decay = sb("decay", [P, 2, NCH])

        bank = ctx.enter_context(nc.psum_tensor("bank", [P, 8, HALF], F32))

        raw_in = [sem(f"raw_in{i}") for i in range(SLOTS)]
        x_in = [sem(f"x_in{t}") for t in range(TT)]
        const_in = sem("const_in")
        g_pre_in, g_post_in, w_al_in = sem("g_pre_in"), sem("g_post_in"), sem("w_al_in")
        second_in = [sem("second_in0"), sem("second_in1")]
        hi_ready, lo_ready, unit_used = sem("hi_ready"), sem("lo_ready"), sem("unit_used")
        a_hi_ready, a_lo_ready = sem("a_hi_ready"), sem("a_lo_ready")
        silu_ready, hidden_ready = sem("silu_ready"), sem("hidden_ready")
        y_done, post_ms, post_ve, post_rstd = sem("y_done"), sem("post_ms"), sem("post_ve"), sem("post_rstd")
        y_scaled, h_new = sem("y_scaled"), sem("h_new")
        pre_ms, pre_ve, pre_rstd = sem("pre_ms"), sem("pre_ve"), sem("pre_rstd")
        normed_ready, uT_ready, uT_hi, uT_lo = sem("normed_ready"), sem("uT_ready"), sem("uT_hi"), sem("uT_lo")
        consts, const_step = sem("consts"), sem("const_step")
        evac = sem("evac")
        z_ready, z_out = sem("z_ready"), sem("z_out")
        f_act, f_dve, c_ready, bias_set = sem("f_act"), sem("f_dve"), sem("c_ready"), sem("bias_set")
        a_act, a_dve = sem("a_act"), sem("a_dve")
        scores_ready, max_ready, exp_done = sem("scores_ready"), sem("max_ready"), sem("exp_done")
        rinv_ready, probs_ready, pt_ready, pt_copied, pv_done = (
            sem("rinv_ready"), sem("probs_ready"), sem("pt_ready"), sem("pt_copied"), sem("pv_done"))
        fox_hi, fox_lo = sem("fox_hi"), sem("fox_lo")
        kst_ready, kst_copied = sem("kst_ready"), sem("kst_copied")
        attn_ready, attn_copied, attn_masked = sem("attn_ready"), sem("attn_copied"), sem("attn_masked")
        intra_zeroed = sem("intra_zeroed")
        kv_ready, state_ready = sem("kv_ready"), sem("state_ready")
        o_ready, sq_ready, gms_ready, gla_act, on_ready = (
            sem("o_ready"), sem("sq_ready"), sem("gms_ready"), sem("gla_act"), sem("on_ready"))
        gr_sig, gr_mul, og_raw, og_hi_ready = sem("gr_sig"), sem("gr_mul"), sem("og_raw"), sem("og_hi_ready")
        merged = sem("merged")
        gate_sig, gate_mul = sem("gate_sig"), sem("gate_mul")
        out_done = sem("out_done")

        steps = [(hh, qb) for hh in range(FOX_H) for qb in range(TT)]
        NS = len(steps)
        gla_steps = [("kst", 0), ("kst", 1)]
        for j in range(2):
            gla_steps += [("attn", 2 * j), ("attn", 2 * j + 1), ("kv", 2 * j), ("kv", 2 * j + 1),
                          ("o", 2 * j), ("ms", 2 * j), ("o", 2 * j + 1), ("ms", 2 * j + 1)]

        cum = scr[:, 2048:2560]

        def feature_bank(u):
            for first, banks in ((U_FK, (1, 2, 3, 4)), (U_FQ, (5, 6, 7, 0)), (U_GQ, (5, 6)), (U_GK, (7, 0))):
                if first <= u < first + len(banks):
                    return banks[u - first]

        def y_tile(t):
            return bank[:, 2 * t:2 * t + 2, :]

        def uT_psum(t):
            return bank[:, 2 * t:2 * t + 2, :].rearrange("p b (k n) -> p (b k) n", k=KD // 2)

        def gain(g):
            return g.rearrange("(o n) -> o n", o=1).to_broadcast([P, D])

        def gbank(g):
            return bank[:, 6 + g % 2, :]

        plain = {}
        for first, count, col in ((U_FK, 4, C_FK), (U_FQ, 4, C_FQ), (U_GQ, 2, C_GQ), (U_GK, 2, C_GK), (U_GR, 4, C_GR)):
            for m in range(count):
                plain[first + m] = col + m * P

        def kmajor(w, cols):
            return w[:, cols].rearrange("(k p) c -> p k c", p=P)

        block = ctx.enter_context(nc.Block())

        @block.sync
        def _(sp):
            def free(u, i=0):
                sp.wait_ge(lo_ready, i + (u - SLOTS + 1))

            def load(u, src, dst=None, i=0):
                free(u, i)
                dst = raw[:, slot(u), :] if dst is None else dst
                sp.dma_start(dst, src).then_inc(raw_in[slot(u)], 16)

            def tiles(u):
                return raw[:, slot(u), :].rearrange("p (k c) -> p k c", k=KD)

            def ffn_loads(u0, wg, wu, wd, peel):
                for j in range(peel):
                    w, f = (wg, wu)[j % 2], j // 2
                    sp.dma_start(tiles(u0 + j), kmajor(w, bass.ds(f * P, P))).then_inc(raw_in[slot(u0 + j)], 16)
                with sp.Fori(peel // 4, KF // 2) as i:
                    for j in range(4):
                        w = (wg, wu)[j % 2]
                        load(u0 + j, kmajor(w, bass.ds(i * 2 * P + (j // 2) * P, P)), tiles(u0 + j), i * 4)
                with sp.Fori(0, KF // 4) as i:
                    for j in range(4):
                        load(u0 + 2 * KF + j, wd[bass.ds(i * 4 * P + j * P, P), :], None, i * 4)
                for k in range(KF // 4 * 4, KF):
                    load(u0 + 2 * KF + k, wd[k * P:(k + 1) * P, :])

            for t in range(TT):
                sp.dma_start(h[:, t, :], x[t * P:(t + 1) * P, :]).then_inc(x_in[t], 16)
            ffn_loads(U_FFN1, w1g, w1u, w1d, SLOTS)

            free(U_SMALL)
            st = raw[:, slot(U_SMALL), 0:KD * SMALL].rearrange("p (k c) -> p k c", k=KD)
            sp.dma_start(st[:, :, 0:FOX_H], kmajor(w_in, slice(C_FL, C_FL + FOX_H))).then_inc(raw_in[slot(U_SMALL)], 16)
            sp.dma_start(st[:, :, ALR:ALR + RANK], kmajor(w_in, slice(C_AL, C_AL + RANK))).then_inc(second_in[0], 16)
            for u in range(U_FK, U_GATE):
                if u == U_FK + 3:
                    sp.wait_ge(y_scaled, TT)
                    sp.dma_start(w_al[ALR:ALR + RANK, :], w_alpha).then_inc(w_al_in, 16)
                if u in plain:
                    load(u, kmajor(w_in, slice(plain[u], plain[u] + P)), tiles(u))
                else:
                    first, col = (U_FV, C_FV) if u < U_GQ else (U_GV, C_GV)
                    k = 2 * (u - first)
                    load(u, w_in[k * P:(k + 2) * P, col:col + N].rearrange("(k p) c -> p k c", p=P),
                         raw[:, slot(u), :].rearrange("p (k c) -> p k c", k=2))
            with sp.Fori(0, KD // 4) as i:
                for m in range(4):
                    u = U_GATE + 3 * m
                    col = i * 4 * P + m * P
                    load(u, kmajor(w_in, bass.ds(col + C_GF, P)), tiles(u), i * 12)
                    load(u + 1, kmajor(w_in, bass.ds(col + C_GG, P)), tiles(u + 1), i * 12)
                    free(u + 2, i * 12)
                    sp.nop(nofuse=True)
                    sp.dma_start(tiles(u + 2)[:, 0:4, :], kmajor(w_bf, bass.ds(col, P))).then_inc(raw_in[slot(u + 2)], 16)
                    sp.dma_start(tiles(u + 2)[:, 4:8, :], kmajor(w_bg, bass.ds(col, P))).then_inc(second_in[m % 2], 16)
            for k in range(KD):
                if k == 2:
                    free(U_OUT + k)
                    for c, arrived in ((0, raw_in[slot(U_OUT + k)]), (HALF, second_in[0])):
                        sp.dma_start(raw[:, slot(U_OUT + k), c:c + HALF],
                                     w_out[k * P:(k + 1) * P, c:c + HALF]).then_inc(arrived, 16)
                else:
                    load(U_OUT + k, w_out[k * P:(k + 1) * P, :])
            ffn_loads(U_FFN2, w2g, w2u, w2d, 0)
            for t in range(TT):
                sp.wait_ge(h_new, 8 + t + 1)
                sp.dma_start(out[t * P:(t + 1) * P, :], h[:, t, :]).then_inc(out_done, 16)
            sp.wait_ge(out_done, 16 * TT)

        @block.scalar
        def _(act):
            consts_dma = [(bias_small[0:FOX_H, :], b_forget.rearrange("(h o) -> h o", o=1)),
                          (bias_alpha[:, :], b_alpha.rearrange("(j p) -> p j", p=P)),
                          (gn[:, :], gla_g.rearrange("(h p) -> p h", p=P))]
            act.wait_ge(bias_set, 1)
            for dst, src in consts_dma:
                act.dma_start(dst, src, allow_slow_non_contiguous=True).then_inc(const_in, 16)

            def split(u, i=0, per=0, second=None):
                act.wait_ge(raw_in[slot(u)], i * (16 * per // SLOTS) + arrivals(u))
                if second is not None:
                    act.wait_ge(*second)
                if not isinstance(i, int) or u + per * i >= SLOTS:
                    act.wait_ge(unit_used, i * per + (u - SLOTS + 1))
                nc.scalar.activation(w_hi[:, slot(u), :], raw[:, slot(u), :], ACT.Copy).then_inc(hi_ready, 1)

            def split_a(u, tile):
                nc.scalar.activation(a_hi[:, slot(u), :], tile, ACT.Copy).then_inc(a_hi_ready, 1)

            squared = []

            def junk_free(mine, count):
                for last in squared:
                    act.wait_ge(*last)
                squared[:] = [(mine, count)]

            def pre_sq(q, t):
                if q < TT:
                    act.wait_ge(x_in[t], 16)
                else:
                    act.wait_ge(h_new, q - TT + 1)
                junk_free(pre_ms, q + 1)
                nc.scalar.activation(junk, h[:, t, :], ACT.Square, scale=D ** -0.5,
                                     accum_out=ms_pre[:, q:q + 1]).then_inc(pre_ms, 1)

            def post_sq(r, t, half):
                if t < TT - 1:
                    act.wait_ge(y_done, (TT - 1) * (r // TT) + t + 1)
                else:
                    act.wait_ge(unit_used, (U_MIX, U_FFN2, U_END)[r // TT])
                junk_free(post_ms, r + 1)
                nc.scalar.activation(junk, y_tile(t), ACT.Square, scale=(2 if half else 1) * D ** -0.5,
                                     accum_out=ms_post[:, r:r + 1]).then_inc(post_ms, 1)

            def uT_evac(q, t):
                act.wait_ge(uT_ready, q + 1)
                nc.scalar.activation(u_hi[:, :, t * P:(t + 1) * P], uT_psum(t), ACT.Copy).then_inc(uT_hi, 1)

            def boundary(b, u_next, small_next=False):
                r, q, half = TT * (b - 1), TT * b, b != 2
                if b == 3:
                    for t in range(TT):
                        post_sq(r + t, t, half)
                    return
                for t in range(3):
                    post_sq(r + t, t, half)
                    pre_sq(q + t, t)
                uT_evac(q, 0)
                post_sq(r + 3, 3, half)
                uT_evac(q + 1, 1)
                split(u_next, second=(second_in[0], 16) if small_next else None)
                pre_sq(q + 3, 3)
                split(u_next + 1)
                uT_evac(q + 2, 2)
                split(u_next + 2)
                uT_evac(q + 3, 3)
                split(u_next + 3)

            def ffn(u0, layer, a0):
                def pair(i, down):
                    for j in range(4):
                        if j % 2 == 0:
                            act.wait_ge(unit_used, i * 4 + (u0 + j + 1))
                            nc.scalar.activation(silu[:, j // 2, :], bank[:, j, :], ACT.Silu).then_inc(silu_ready, 1)
                        split(u0 + j + 4, i, 4)
                        if down:
                            split_a(u0 + j + 4, arena[:, j, :])

                with act.Fori(0, KF // 2 - 1) as i:
                    pair(i, False)
                act.wait_ge(hidden_ready, PAIRS + layer * KF + 4)
                pair(KF // 2 - 1, True)
                ud = u0 + 2 * KF
                with act.Fori(0, 4) as i:
                    for j in range(4):
                        split(ud + j + 4, i, 4)
                        act.wait_ge(hidden_ready, i * 4 + (PAIRS + layer * KF + j + 5))
                        split_a(ud + j + 4, arena[:, bass.ds(i * 4 + (j + 4), 1), :])
                for k in (20, 21):
                    split(ud + k)
                    act.wait_ge(hidden_ready, PAIRS + layer * KF + k + 1)
                    split_a(ud + k, arena[:, k, :])

            pre_sq(0, 0)
            pre_sq(1, 1)
            pre_sq(2, 2)
            uT_evac(0, 0)
            pre_sq(3, 3)
            uT_evac(1, 1)
            split(0)
            uT_evac(2, 2)
            split(1)
            uT_evac(3, 3)
            split(2)
            split(3)
            ffn(U_FFN1, 0, A_FFN1)
            boundary(1, U_MIX, small_next=True)

            act.wait_ge(const_in, 16 * len(consts_dma))
            for s in range(21):
                v = U_MIX + s
                act.wait_ge(unit_used, v + 1)
                if s == 0:
                    nc.scalar.activation(small[0:SMALL, :], bank[0:SMALL, 0, :], ACT.Identity,
                                         bias=bias_small[:, :]).then_inc(evac, 1)
                elif v in plain:
                    dst, m = [(d, v - f) for f, n, d in ((U_FK, 4, T_K), (U_FQ, 4, T_Q), (U_GQ, 2, T_GQ), (U_GK, 2, T_GK))
                              if f <= v < f + n][0]
                    nc.scalar.activation(arena[:, dst + m, :], bank[:, feature_bank(v), :], ACT.Copy,
                                         scale=0.125 if dst in (T_Q, T_GQ) else 1.0).then_inc(evac, 1)
                elif v in (U_FV + 3, U_GV + 3):
                    for t in range(TT):
                        nc.scalar.activation(arena[:, (T_V if v < U_GQ else T_GV) + t, :], bank[:, 1 + t, :],
                                             ACT.Copy).then_inc(evac, 1)
                if s == 1:
                    act.wait_ge(evac, 1)
                    nc.scalar.activation(fsum[0:FOX_H, :], small[0:FOX_H, :], ACT.Abs).then_inc(f_act, 1)
                    act.wait_ge(f_act, 1)
                    nc.scalar.activation(fsum[0:FOX_H, :], fsum[0:FOX_H, :], ACT.Exp, scale=-1.0).then_inc(f_act, 1)
                    act.wait_ge(f_act, 2)
                    nc.scalar.activation(fsum[0:FOX_H, :], fsum[0:FOX_H, :], ACT.Ln, bias=1.0).then_inc(f_act, 1)
                if s == 3:
                    for j in range(2):
                        act.wait_ge(z_ready, j + 1)
                        nc.scalar.activation(ga[:, j, :], bank[:, 6 + j, :], ACT.Identity,
                                             bias=bias_alpha[:, j:j + 1]).then_inc(z_out, 1)
                if s == 4:
                    act.wait_ge(z_out, 2)
                    nc.scalar.activation(gb, ga, ACT.Abs).then_inc(a_act, 1)
                    act.wait_ge(a_act, 1)
                    nc.scalar.activation(gb, gb, ACT.Exp, scale=-1.0).then_inc(a_act, 1)
                    act.wait_ge(a_act, 2)
                    nc.scalar.activation(gb, gb, ACT.Ln, bias=1.0).then_inc(a_act, 1)
                if s == 5:
                    act.wait_ge(a_dve, 2)
                    nc.scalar.activation(ga, gb, ACT.Exp, scale=1.0 / TAU).then_inc(a_act, 1)
                if s == 6:
                    act.wait_ge(a_dve, 3)
                    kst = arena[:, T_KST:T_KST + 2, :]
                    nc.scalar.activation(kst, kst, ACT.Exp, scale=1.0 / TAU).then_inc(a_act, 1)
                if s == 15:
                    act.wait_ge(a_dve, 5)
                    nc.scalar.activation(ga, gb, ACT.Exp, scale=-1.0 / TAU).then_inc(a_act, 1)
                split(v + 4)

            for sl in range(NS + 2):
                if sl < NS:
                    hh, qb = steps[sl]
                    kend = (qb + 1) * P
                    act.wait_ge(max_ready, sl + 1)
                    if sl >= 2:
                        act.wait_ge(pt_ready, sl - 1)
                    nc.scalar.activation(probs[:, sl % 2, 0:kend], bank[:, sl % 2, 0:kend], ACT.Exp,
                                         bias=neg_max[:, sl:sl + 1],
                                         accum_out=rowsum[:, sl:sl + 1]).then_inc(exp_done, 1)
                if 1 <= sl <= NS:
                    s = sl - 1
                    kend = (steps[s][1] + 1) * P
                    act.wait_ge(pt_ready, s + 1)
                    if s >= 2:
                        act.wait_ge(pv_done, s - 1)
                    nc.scalar.activation(probsT[:, s % 2, 0:kend], bank[:, 2 + s % 2, 0:kend],
                                         ACT.Copy).then_inc(pt_copied, 1)
                if sl >= 9 and (sl - 9) % 8 == 0:
                    p = (sl - 9) // 8
                    act.wait_ge(pv_done, 8 * p + 8)
                    nc.scalar.activation(of_hi[:, p, :], bank[:, 4 + p % 2, :], ACT.Copy).then_inc(fox_hi, 1)
                if sl < len(gla_steps):
                    kind, n = gla_steps[sl]
                    if kind == "kst" and n == 1:
                        act.wait_ge(kst_ready, 2)
                        for i in range(2):
                            nc.scalar.activation(kst_tok[:, 2 * i:2 * i + 2, :].rearrange("p t f -> p (t f)"),
                                                 gbank(i), ACT.Copy).then_inc(kst_copied, 1)
                    if kind == "attn":
                        act.wait_ge(attn_ready, n + 1)
                        act.wait_ge(intra_zeroed, 1)
                        if n >= 2:
                            act.wait_ge(o_ready, n - 1)
                        src = gbank(sl).rearrange("p (t c) -> p t c", t=TT)
                        for c in range(2):
                            rows = slice(c * CHUNK, (c + 1) * CHUNK)
                            nc.scalar.activation(intra[rows, n % 2, :, rows], src[rows, :, rows], ACT.Copy).then_inc(attn_copied, 1)
                    if kind == "o":
                        act.wait_ge(o_ready, n + 1)
                        if n >= 2:
                            act.wait_ge(gms_ready, n - 1)
                        nc.scalar.activation(sq[:, n % 2, :], gbank(sl), ACT.Square).then_inc(sq_ready, 1)
                    if kind == "ms":
                        act.wait_ge(gms_ready, n + 1)
                        if n >= 2:
                            act.wait_ge(on_ready, n - 1)
                        nc.scalar.activation(rstd_g[:, n % 2, :], gbank(sl), ACT.Ln, bias=eps_t[:, :]).then_inc(gla_act, 1)
                        act.wait_ge(gla_act, 2 * n + 1)
                        nc.scalar.activation(rstd_g[:, n % 2, :], rstd_g[:, n % 2, :], ACT.Exp,
                                             scale=-0.5).then_inc(gla_act, 1)

            for hh in range(GLA_H + 1):
                if hh < GLA_H:
                    act.wait_ge(unit_used, U_GR + hh + 1)
                    nc.scalar.activation(sig[:, hh, :], bank[:, hh, :], ACT.Sigmoid).then_inc(gr_sig, 1)
                    split(U_GR + hh + 4, second=(second_in[0], 32) if hh == 2 else None)
                if hh >= 1:
                    act.wait_ge(og_raw, hh)
                    nc.scalar.activation(og_hi[:, hh - 1, :], arena[:, T_OG[hh - 1], :], ACT.Copy).then_inc(og_hi_ready, 1)

            act.wait_ge(merged, GLA_H)
            with act.Fori(0, KD // 4) as i:
                for m in range(4):
                    for j in range(3):
                        v = U_GATE + 3 * m + j
                        if j < 2:
                            act.wait_ge(unit_used, i * 12 + (v + 1))
                            nc.scalar.activation(sig[:, 2 * (m % 2) + j, :], bank[:, 4 * ((m + 1) % 2) + j, :],
                                                 ACT.Sigmoid).then_inc(gate_sig, 1)
                        k = 3 * m + j + 4
                        mm = k // 3
                        second = (second_in[mm % 2], i * 32 + 16 * (mm // 2 + 1 + (mm + 1) % 2)) if k % 3 == 2 else None
                        split(v + 4, i, 12, second)

            act.wait_ge(unit_used, U_OUT)
            for k in range(4):
                act.wait_ge(merged, GLA_H + k + 1)
                split_a(U_OUT + k, arena[:, k, :])
            act.wait_ge(merged, GLA_H + KD)
            for k in range(4, KD):
                split(U_OUT + k)
                split_a(U_OUT + k, arena[:, k, :])
            boundary(2, U_FFN2)
            ffn(U_FFN2, 1, A_FFN2)
            boundary(3, None)

        @block.vector
        def _(dve):
            V = nc.vector

            def split(u, i=0, per=0):
                dve.wait_ge(hi_ready, i * per + (u + 1))
                V.tensor_tensor(w_lo[:, slot(u), :], raw[:, slot(u), :], w_hi[:, slot(u), :].bitcast(F32),
                                ALU.subtract).then_inc(lo_ready, 1)

            def split_a(a, u, tile, i=0):
                dve.wait_ge(a_hi_ready, i * 4 + (a + 1))
                V.tensor_tensor(a_lo[:, slot(u), :], tile, a_hi[:, slot(u), :].bitcast(F32),
                                ALU.subtract).then_inc(a_lo_ready, 1)

            def norm_in(q, t):
                dve.wait_ge(pre_rstd, q + 1)
                if t == 0:
                    dve.wait_ge(g_pre_in, 16 * (q // TT + 1))
                if q >= TT:
                    dve.wait_ge(h_new, q - TT + 1)
                if q >= 2:
                    dve.wait_ge(uT_ready, q - 1)
                V.scalar_tensor_tensor(normed[:, q % 2, :], h[:, t, :], rstd_pre[:, q:q + 1], g_pre,
                                       ALU.mult, ALU.mult).then_inc(normed_ready, 1)

            def uT_rest(q, t):
                dve.wait_ge(uT_hi, q + 1)
                cols = slice(t * P, (t + 1) * P)
                V.tensor_tensor(u_lo[:, :, cols], uT_psum(t), u_hi[:, :, cols].bitcast(F32),
                                ALU.subtract).then_inc(uT_lo, 1)

            def residual(r, t):
                dve.wait_ge(post_rstd, r + 1)
                if t == 0:
                    dve.wait_ge(g_post_in, 16 * (r // TT + 1))
                if r >= 1:
                    dve.wait_ge(h_new, r)
                V.scalar_tensor_tensor(scaled, y_tile(t), rstd_post[:, r:r + 1],
                                       g_post.rearrange("p (b n) -> p b n", b=2), ALU.mult, ALU.mult).then_inc(y_scaled, 1)
                dve.wait_ge(y_scaled, r + 1)
                V.tensor_tensor(h[:, t, :], h[:, t, :], scaled, ALU.add).then_inc(h_new, 1)

            def boundary(b, u_next):
                r, q = TT * (b - 1), TT * b
                if b == 3:
                    for t in range(TT):
                        residual(r + t, t)
                    return
                for t in range(3):
                    residual(r + t, t)
                    norm_in(q + t, t)
                uT_rest(q, 0)
                residual(r + 3, 3)
                uT_rest(q + 1, 1)
                split(u_next)
                norm_in(q + 3, 3)
                split(u_next + 1)
                uT_rest(q + 2, 2)
                split(u_next + 2)
                uT_rest(q + 3, 3)
                split(u_next + 3)

            def ffn(u0, layer, a0):
                def pair(i, down):
                    for j in range(4):
                        if j % 2:
                            dve.wait_ge(unit_used, i * 4 + (u0 + j + 1))
                            dve.wait_ge(silu_ready, i * 2 + (layer * KF + j // 2 + 1))
                            f = (bass.ds(i * 2 + j // 2, 1))
                            V.tensor_tensor(arena[:, f, :], silu[:, j // 2, :].rearrange("p (o n) -> p o n", o=1),
                                            bank[:, j:j + 1, :], ALU.mult).then_inc(hidden_ready, 1)
                        split(u0 + j + 4, i, 4)
                        if down:
                            split_a(a0 + j, u0 + j + 4, arena[:, j, :])

                with dve.Fori(0, KF // 2 - 1) as i:
                    pair(i, False)
                dve.wait_ge(hidden_ready, PAIRS + layer * KF + 4)
                pair(KF // 2 - 1, True)
                ud = u0 + 2 * KF
                with dve.Fori(0, 4) as i:
                    for j in range(4):
                        split(ud + j + 4, i, 4)
                        dve.wait_ge(hidden_ready, i * 4 + (PAIRS + layer * KF + j + 5))
                        split_a(a0 + j + 4, ud + j + 4, arena[:, bass.ds(i * 4 + (j + 4), 1), :].rearrange("p o n -> p (o n)"), i)
                for k in (20, 21):
                    split(ud + k)
                    dve.wait_ge(hidden_ready, PAIRS + layer * KF + k + 1)
                    split_a(a0 + k, ud + k, arena[:, k, :])

            V.memset(bias_small[:, :], 0.0).then_inc(bias_set, 1)
            V.memset(ones[:, :], 1.0)
            V.memset(eps_t[:, :], EPS)
            V.memset(c_parts[:, :].bitcast(F32), 0.0)
            V.memset(mean_g[:, :], 1.0 / GLA_DV).then_inc(hidden_ready, PAIRS)
            dve.wait_ge(const_step, 10)
            V.tensor_copy(ident_r[:, :], ident[:, :])
            V.tensor_copy(causal[:, :], arena[:, 0, 0:P])
            V.tensor_copy(head_sel[:, :, :].rearrange("p h o -> p (h o)"), arena[0:CROWS, 1, 0:2 * FOX_H]).then_inc(consts, 1)

            norm_in(0, 0)
            norm_in(1, 1)
            uT_rest(0, 0)
            norm_in(2, 2)
            norm_in(3, 3)
            uT_rest(1, 1)
            split(0)
            uT_rest(2, 2)
            split(1)
            uT_rest(3, 3)
            split(2)
            split(3)
            ffn(U_FFN1, 0, A_FFN1)
            boundary(1, U_MIX)

            for s in range(21):
                v = U_MIX + s
                if s == 1:
                    dve.wait_ge(f_act, 3)
                    V.scalar_tensor_tensor(fsum[0:FOX_H, :], small[0:FOX_H, :], 0.0, fsum[0:FOX_H, :],
                                           ALU.min, ALU.subtract).then_inc(f_dve, 1)
                    dve.wait_ge(f_dve, 1)
                    V.tensor_tensor_scan(cum[0:FOX_H, :], ones[0:FOX_H, 0:1].to_broadcast([FOX_H, N]), fsum[0:FOX_H, :],
                                         0.0, ALU.mult, ALU.add).then_inc(f_dve, 1)
                    dve.wait_ge(f_dve, 2)
                    for r in (0, 64):
                        last = V.tensor_copy(c_parts[r:r + FOX_H, :], cum[0:FOX_H, :])
                    last.then_inc(f_dve, 1)
                    dve.wait_ge(f_dve, 3)
                    for r in (32, 96):
                        last = V.tensor_tensor(c_parts[r:r + FOX_H, :], cum[0:FOX_H, :], c_parts[0:FOX_H, :].bitcast(F32),
                                               ALU.subtract)
                    last.then_inc(f_dve, 1)
                    dve.wait_ge(f_dve, 4)
                    V.tensor_scalar(c_neg[:, :], c_parts[:, :].bitcast(F32), -1.0, None, ALU.mult).then_inc(c_ready, 1)
                if s == 4:
                    dve.wait_ge(a_act, 3)
                    V.scalar_tensor_tensor(ga, ga, 0.0, gb, ALU.min, ALU.subtract).then_inc(a_dve, 1)
                    dve.wait_ge(a_dve, 1)
                    for j in range(2):
                        for n in range(NCH):
                            cols = slice(n * CHUNK, (n + 1) * CHUNK)
                            last = V.tensor_tensor_scan(gb[:, j, cols], ones[:, 0:1].to_broadcast([P, CHUNK]), ga[:, j, cols],
                                                        0.0, ALU.mult, ALU.add)
                    last.then_inc(a_dve, 1)
                if s == 5:
                    dve.wait_ge(a_dve, 2)
                    for j in range(2):
                        bj = gb[:, j, :].rearrange("p (n c) -> p n c", n=NCH)
                        last = V.tensor_tensor(arena[:, T_KST + j, :].rearrange("p (n c) -> p n c", n=NCH),
                                               bj[:, :, CHUNK - 1:CHUNK].to_broadcast([P, NCH, CHUNK]), bj, ALU.subtract)
                    last.then_inc(a_dve, 1)
                    dve.wait_ge(a_act, 4)
                    ends = ga.rearrange("p j (n c) -> p j n c", n=NCH)[:, :, :, CHUNK - 1]
                    V.tensor_copy(decay[:, :, :], ends).then_inc(a_dve, 1)
                if s == 14:
                    dve.wait_ge(evac, 15)
                    qin = arena[:, T_GQ:T_GQ + 2, :]
                    V.tensor_tensor(qin, qin, ga, ALU.mult).then_inc(a_dve, 1)
                if s == 16:
                    dve.wait_ge(evac, 17)
                    dve.wait_ge(a_act, 5)
                    kin, kst = arena[:, T_GK:T_GK + 2, :], arena[:, T_KST:T_KST + 2, :]
                    V.tensor_tensor(kst, kst, kin, ALU.mult).then_inc(a_dve, 1)
                    dve.wait_ge(a_act, 6)
                    V.tensor_tensor(kin, kin, ga, ALU.mult).then_inc(a_dve, 1)
                split(v + 4)

            for sl in range(NS + 2):
                if sl < NS:
                    kend = (steps[sl][1] + 1) * P
                    dve.wait_ge(scores_ready, sl + 1)
                    V.tensor_reduce(neg_max[:, sl:sl + 1], bank[:, sl % 2, 0:kend], AX.X, ALU.max,
                                    negate=True).then_inc(max_ready, 1)
                if 1 <= sl <= NS:
                    s = sl - 1
                    kend = (steps[s][1] + 1) * P
                    dve.wait_ge(exp_done, s + 1)
                    V.reciprocal(rinv[:, s:s + 1], rowsum[:, s:s + 1]).then_inc(rinv_ready, 1)
                    dve.wait_ge(rinv_ready, s + 1)
                    V.tensor_scalar(probs[:, s % 2, 0:kend], probs[:, s % 2, 0:kend], rinv[:, s:s + 1], None,
                                    ALU.mult).then_inc(probs_ready, 1)
                if sl >= 9 and (sl - 9) % 8 == 0:
                    p = (sl - 9) // 8
                    dve.wait_ge(fox_hi, p + 1)
                    V.tensor_tensor(of_lo[:, p, :], bank[:, 4 + p % 2, :], of_hi[:, p, :].bitcast(F32),
                                    ALU.subtract).then_inc(fox_lo, 1)
                if sl < len(gla_steps):
                    kind, n = gla_steps[sl]
                    if kind == "kv" and n % 2:
                        j = n // 2
                        dve.wait_ge(kv_ready, n + 1)
                        if j:
                            dve.wait_ge(o_ready, 2)
                        for c in range(NCH - 1):
                            kv = gbank(sl - 1 + c % 2)[:, (c // 2) * GLA_DV:(c // 2 + 1) * GLA_DV]
                            if c == 0:
                                V.tensor_copy(state[:, 1, :], kv).then_inc(state_ready, 1)
                            else:
                                dve.wait_ge(state_ready, j * (NCH - 1) + c)
                                V.scalar_tensor_tensor(state[:, c + 1, :], state[:, c, :], decay[:, j, c:c + 1],
                                                       kv, ALU.mult, ALU.add).then_inc(state_ready, 1)
                    if kind == "ms":
                        dve.wait_ge(gla_act, 2 * n + 2)
                        V.scalar_tensor_tensor(arena[:, T_OG[n], :], gbank(sl - 1), gn[:, n:n + 1], rstd_g[:, n % 2, :],
                                               ALU.mult, ALU.mult).then_inc(on_ready, 1)

            for hh in range(GLA_H):
                dve.wait_ge(gr_sig, hh + 1)
                V.tensor_tensor(part[:, hh, :], sig[:, hh, :], bank[:, hh, :], ALU.mult).then_inc(gr_mul, 1)
                dve.wait_ge(gr_mul, hh + 1)
                dve.wait_ge(on_ready, hh + 1)
                tile = arena[:, T_OG[hh], :]
                V.tensor_tensor(tile, tile, part[:, hh, :], ALU.mult).then_inc(og_raw, 1)
                split(U_GR + hh + 4)
                dve.wait_ge(og_hi_ready, hh + 1)
                V.tensor_tensor(og_lo[:, hh, :], tile, og_hi[:, hh, :].bitcast(F32), ALU.subtract).then_inc(merged, 1)

            with dve.Fori(0, KD // 4) as i:
                for m in range(4):
                    b0, s0 = 4 * ((m + 1) % 2), 2 * (m % 2)
                    v = U_GATE + 3 * m
                    split(v + 4, i, 12)
                    split(v + 5, i, 12)
                    dve.wait_ge(gate_sig, i * 8 + (2 * m + 2))
                    dve.wait_ge(unit_used, i * 12 + (v + 3))
                    V.tensor_tensor(part[:, s0:s0 + 2, :], sig[:, s0:s0 + 2, :], bank[:, b0 + 2:b0 + 4, :],
                                    ALU.mult).then_inc(gate_mul, 1)
                    dve.wait_ge(gate_mul, i * 4 + (m + 1))
                    V.tensor_tensor(arena[:, bass.ds(i * 4 + m, 1), :], part[:, s0:s0 + 1, :], part[:, s0 + 1:s0 + 2, :],
                                    ALU.add).then_inc(merged, 1)
                    split(v + 6, i, 12)

            for k in range(4):
                dve.wait_ge(merged, GLA_H + k + 1)
                split_a(A_OUT + k, U_OUT + k, arena[:, k, :])
            dve.wait_ge(merged, GLA_H + KD)
            for k in range(4, KD):
                split(U_OUT + k)
                split_a(A_OUT + k, U_OUT + k, arena[:, k, :])
            boundary(2, U_FFN2)
            ffn(U_FFN2, 1, A_FFN2)
            boundary(3, None)

        @block.tensor
        def _(pe):
            mm = nc.tensor.matmul

            def weights(u, i=0, per=0):
                pe.wait_ge(lo_ready, i * per + (u + 1))

            def feature_product(u, dst, k_tiles=range(KD), rhs_hi=None, rhs_lo=None):
                rhs_hi, rhs_lo = (u_hi, u_lo) if rhs_hi is None else (rhs_hi, rhs_lo)
                k0, k1 = k_tiles[0], k_tiles[-1]
                for k in k_tiles:
                    w = slice(k * P, (k + 1) * P)
                    mm(dst, w_hi[:, slot(u), w], rhs_hi[:, k - k0, :], start=k == k0, stop=False)
                    mm(dst, w_hi[:, slot(u), w], rhs_lo[:, k - k0, :], start=False, stop=False)
                    last = mm(dst, w_lo[:, slot(u), w], rhs_hi[:, k - k0, :], start=False, stop=k == k1)
                return last

            def token_product(u, t, first, final):
                s, toks = slot(u), slice(t * P, (t + 1) * P)
                for a, w in ((a_hi, w_hi), (a_hi, w_lo), (a_lo, w_hi)):
                    for c in range(2):
                        last = mm(bank[:, 2 * t + c, :], a[:, s, toks], w[:, s, c * HALF:(c + 1) * HALF],
                                  start=first and a is a_hi and w is w_hi, stop=final and a is a_lo)
                return last

            def transposes(q, t):
                pe.wait_ge(normed_ready, q + 1)
                for k in range(KD):
                    last = nc.tensor.transpose(bank[:, 2 * t + k // 4, (k % 4) * P:(k % 4 + 1) * P],
                                               normed[:, q % 2, k * P:(k + 1) * P], ident[:, :])
                last.then_inc(uT_ready, 1)

            def last_units(b, u0, a0):
                q = TT * b
                for t in range(TT):
                    for k in range(4):
                        if t == 0:
                            weights(u0 + k)
                            pe.wait_ge(a_lo_ready, a0 + k + 1)
                        last = token_product(u0 + k, t, False, k == 3)
                        if t == TT - 1:
                            last.then_inc(unit_used, 1)
                    if t < TT - 1:
                        last.then_inc(y_done, 1)
                    if b < 3 and t == 2:
                        transposes(q, 0)
                if b < 3:
                    for t in range(1, TT):
                        transposes(q + t, t)

            def ffn(u0, layer, a0, b):
                pe.wait_ge(uT_lo, TT * (b - 1) + TT)
                with pe.Fori(0, KF // 2) as i:
                    for j in range(4):
                        if j % 2 == 0:
                            pe.wait_ge(hidden_ready, i * 2 + (layer * KF + j // 2 + 1))
                        weights(u0 + j, i, 4)
                        feature_product(u0 + j, bank[:, j, :]).then_inc(unit_used, 1)
                ud = u0 + 2 * KF

                def down(k, i=0, first=False):
                    weights(ud + k, i, 4)
                    pe.wait_ge(a_lo_ready, i * 4 + (a0 + k + 1))
                    for n, t in enumerate((0, 2, 3, 1)):
                        if first and t < 2:
                            pe.wait_ge(hidden_ready, PAIRS + layer * KF + KF - 1 + t)
                        last = token_product(ud + k, t, first, False)
                    last.then_inc(unit_used, 1)

                for k in range(4):
                    down(k, first=k == 0)
                with pe.Fori(0, 3) as i:
                    for j in range(4, 8):
                        down(j, i)
                down(16)
                down(17)
                last_units(b, ud + 18, a0 + 18)

            pe.wait_ge(consts, 1)
            for t in range(TT):
                transposes(t, t)
            ffn(U_FFN1, 0, A_FFN1, 1)

            pe.wait_ge(uT_lo, 2 * TT)
            bank_evac = {U_FQ + 3: 1, U_FV: 5, U_GQ: 6, U_GQ + 1: 7, U_GK: 8, U_GK + 1: 9, U_GV: 13}
            for s in range(21):
                v = U_MIX + s
                weights(v)
                if v in bank_evac:
                    pe.wait_ge(evac, bank_evac[v])
                if v in (U_FQ + 1, U_FQ + 2):
                    pe.wait_ge(z_out, v - U_FQ)
                if s == 0:
                    sm = slot(v)
                    for k in range(KD):
                        w = slice(k * SMALL, (k + 1) * SMALL)
                        mm(bank[0:SMALL, 0, :], w_hi[:, sm, w], u_hi[:, k, :], start=k == 0, stop=False)
                        mm(bank[0:SMALL, 0, :], w_hi[:, sm, w], u_lo[:, k, :], start=False, stop=False)
                        last = mm(bank[0:SMALL, 0, :], w_lo[:, sm, w], u_hi[:, k, :], start=False, stop=k == KD - 1)
                elif v in plain:
                    last = feature_product(v, bank[:, feature_bank(v), :])
                else:
                    first = U_FV if v < U_GQ else U_GV
                    for kk in range(2):
                        k = 2 * (v - first) + kk
                        w = slice(kk * HALF, (kk + 1) * HALF)
                        for t in range(TT):
                            toks = slice(t * P, (t + 1) * P)
                            dst = bank[:, 1 + t, :]
                            mm(dst, u_hi[:, k, toks], w_hi[:, slot(v), w], start=k == 0, stop=False)
                            mm(dst, u_hi[:, k, toks], w_lo[:, slot(v), w], start=False, stop=False)
                            last = mm(dst, u_lo[:, k, toks], w_hi[:, slot(v), w], start=False, stop=k == KD - 1)
                last.then_inc(unit_used, 1)
                if s == 2:
                    pe.wait_ge(evac, 1)
                    pe.wait_ge(w_al_in, 16)
                    for j in range(2):
                        mm(bank[:, 6 + j, :], w_al[ALR:ALR + RANK, j * P:(j + 1) * P], small[ALR:ALR + RANK, :],
                           start=True, stop=True).then_inc(z_ready, 1)

            pe.wait_ge(evac, 21)
            pe.wait_ge(c_ready, 1)
            pe.wait_ge(a_dve, 7)
            read = {"kst": lambda n: (kst_copied, n + 1), "attn": lambda n: (attn_copied, 2 * n + 2),
                    "kv": lambda n: (state_ready, (NCH - 1) * (n // 2 + 1)), "o": lambda n: (on_ready, n + 1),
                    "ms": lambda n: (gla_act, 2 * n + 1)}
            for sl in range(NS + 2):
                if sl < NS:
                    hh, qb = steps[sl]
                    kend, rows, toks = (qb + 1) * P, slice(64 * (hh % 2), 64 * (hh % 2) + 64), slice(qb * P, (qb + 1) * P)
                    dst = bank[:, sl % 2, 0:kend]
                    if sl >= 2:
                        pe.wait_ge(exp_done, sl - 1)
                    mm(dst, arena[rows, T_Q + hh // 2, toks], arena[rows, T_K + hh // 2, 0:kend], start=True, stop=False)
                    crows = slice(rows.start, rows.start + 32 + FOX_H)
                    sel_h = head_sel[crows, hh, 0:1]
                    mm(dst, c_parts[crows, toks], sel_h.to_broadcast([32 + FOX_H, kend]), start=False, stop=False)
                    mm(dst, sel_h.to_broadcast([32 + FOX_H, P]), c_neg[crows, 0:kend], start=False, stop=False)
                    mm(bank[:, sl % 2, qb * P:kend], ident_r[:, :], causal[:, :], start=False, stop=True).then_inc(scores_ready, 1)
                if 1 <= sl <= NS:
                    s = sl - 1
                    pe.wait_ge(probs_ready, s + 1)
                    if s >= 2:
                        pe.wait_ge(pt_copied, s - 1)
                    for kb in range(steps[s][1] + 1):
                        cols = slice(kb * P, (kb + 1) * P)
                        last = nc.tensor.transpose(bank[:, 2 + s % 2, cols], probs[:, s % 2, cols], ident[:, :])
                    last.then_inc(pt_ready, 1)
                if sl >= 2:
                    s = sl - 2
                    hh, qb = steps[s]
                    pair = hh // 2
                    pe.wait_ge(pt_copied, s + 1)
                    if s % 8 == 0 and pair >= 2:
                        pe.wait_ge(fox_lo, pair - 1)
                    for kb in range(qb + 1):
                        last = mm(bank[64 * (hh % 2):64 * (hh % 2) + 64, 4 + pair % 2, qb * P:(qb + 1) * P],
                                  arena[:, T_V + kb, hh * FOX_D:(hh + 1) * FOX_D], probsT[:, s % 2, kb * P:(kb + 1) * P],
                                  start=kb == 0, stop=kb == qb)
                    last.then_inc(pv_done, 1)
                if sl < len(gla_steps):
                    kind, n = gla_steps[sl]
                    if sl >= 2:
                        pk, pn = gla_steps[sl - 2]
                        pe.wait_ge(*read[pk](pn))
                    dst = gbank(sl)
                    if kind == "kst":
                        for t in (2 * n, 2 * n + 1):
                            for j in range(2):
                                c = (t % 2) * 2 * P + j * P
                                last = nc.tensor.transpose(dst[:, c:c + P], arena[:, T_KST + j, t * P:(t + 1) * P], ident[:, :])
                        last.then_inc(kst_ready, 1)
                    if kind == "attn":
                        rows = slice(64 * (n % 2), 64 * (n % 2) + 64)
                        for t in range(TT):
                            toks = slice(t * P, (t + 1) * P)
                            last = mm(dst[:, toks], arena[rows, T_GK + n // 2, toks], arena[rows, T_GQ + n // 2, toks],
                                      start=True, stop=True)
                        last.then_inc(attn_ready, 1)
                    if kind == "kv":
                        j, part_n = n // 2, n % 2
                        pe.wait_ge(kst_copied, 2)
                        for c in range(part_n, NCH - 1, 2):
                            rows = slice(CHUNK * part_n, CHUNK * part_n + CHUNK)
                            for e in range(2):
                                hh = 2 * j + e
                                last = mm(dst[64 * e:64 * e + 64, (c // 2) * P:(c // 2 + 1) * P],
                                          kst_tok[rows, c // 2, hh * GLA_DK:(hh + 1) * GLA_DK],
                                          arena[rows, T_GV + c // 2, hh * GLA_DV:(hh + 1) * GLA_DV], start=True, stop=True)
                        last.then_inc(kv_ready, 1)
                    if kind == "o":
                        pe.wait_ge(attn_masked, 2 * n + 2)
                        pe.wait_ge(state_ready, (NCH - 1) * (n // 2 + 1))
                        rows_k = slice(64 * (n % 2), 64 * (n % 2) + 64)
                        for t in range(TT):
                            mm(dst[:, t * P:(t + 1) * P], arena[:, T_GV + t, n * GLA_DV:(n + 1) * GLA_DV],
                               intra[:, n % 2, t, :], start=True, stop=False)
                            for c in (2 * t, 2 * t + 1):
                                if c:
                                    cols = slice(c * CHUNK, (c + 1) * CHUNK)
                                    last = mm(dst[:, cols], state[rows_k, c, :], arena[rows_k, T_GQ + n // 2, cols],
                                              start=False, stop=c % 2 == 1)
                        last.then_inc(o_ready, 1)
                    if kind == "ms":
                        pe.wait_ge(sq_ready, n + 1)
                        mm(dst, mean_g[:, :], sq[:, n % 2, :], start=True, stop=True).then_inc(gms_ready, 1)

            for hh in range(GLA_H):
                weights(U_GR + hh)
                feature_product(U_GR + hh, bank[:, hh, :]).then_inc(unit_used, 1)

            with pe.Fori(0, KD // 4) as i:
                for m in range(4):
                    b0, v = 4 * ((m + 1) % 2), U_GATE + 3 * m
                    pe.wait_ge(merged, i * 4 + (m + 3))
                    for j in range(2):
                        weights(v + j, i, 12)
                        feature_product(v + j, bank[:, b0 + j, :]).then_inc(unit_used, 1)
                    weights(v + 2, i, 12)
                    pe.wait_ge(merged, GLA_H)
                    feature_product(v + 2, bank[:, b0 + 2, :], range(4), of_hi, of_lo)
                    feature_product(v + 2, bank[:, b0 + 3, :], range(4, 8), og_hi, og_lo).then_inc(unit_used, 1)

            for k in range(4):
                weights(U_OUT + k)
                pe.wait_ge(a_lo_ready, A_OUT + k + 1)
                for t in (2, 3, 0, 1):
                    if k == 0:
                        pe.wait_ge(merged, GLA_H + (KD - 1 if t >= 2 else KD))
                    last = token_product(U_OUT + k, t, k == 0, False)
                last.then_inc(unit_used, 1)
            last_units(2, U_OUT + 4, A_OUT + 4)
            ffn(U_FFN2, 1, A_FFN2, 3)

        @block.gpsimd
        def _(pool):
            G = nc.gpsimd
            G.dma_start(g_pre, gain(g1pre)).then_inc(g_pre_in, 16)
            G.dma_start(g_post, gain(g1post)).then_inc(g_post_in, 16)
            G.memset(half_neg[:, :], -0.5).then_inc(const_step, 1)
            G.memset(ident[:, :], 0.0).then_inc(const_step, 1)
            G.memset(arena[:, 0, 0:P], 0.0).then_inc(const_step, 1)
            sel = arena[0:CROWS, 1, 0:2 * FOX_H]
            G.memset(sel, 0.0).then_inc(const_step, 1)
            pool.wait_ge(const_step, 4)
            G.affine_select(out=ident[:, :], in_=ident[:, :], compare_op=ALU.not_equal, fill=1.0, base=0,
                            pattern=[[-1, P]], channel_multiplier=1).then_inc(const_step, 1)
            G.affine_select(out=arena[:, 0, 0:P], in_=arena[:, 0, 0:P], compare_op=ALU.is_ge, fill=MASKED, base=0,
                            pattern=[[-1, P]], channel_multiplier=1).then_inc(const_step, 1)
            selv = sel.rearrange("p (h o) -> p h o", o=2)
            for n in range(4):
                if n:
                    pool.wait_ge(const_step, 6 + n)
                G.affine_select(out=selv, in_=selv, compare_op=ALU.not_equal, fill=1.0, base=-32 * n,
                                pattern=[[-1, FOX_H], [0, 2]], channel_multiplier=1).then_inc(const_step, 1)

            def rsqrt(arrived, n, ms, ve, rstd, stepped, ready, eps):
                pool.wait_ge(arrived, n + 1)
                c = slice(n, n + 1)
                G.tensor_scalar(ve[:, c], ms[:, c], eps, None, ALU.add).then_inc(stepped, 1)
                pool.wait_ge(stepped, n + 1)
                G.tensor_tensor(rstd[:, c], ve[:, c], half_neg[:, :], ALU.pow).then_inc(ready, 1)

            def pre(n):
                rsqrt(pre_ms, n, ms_pre, ve_pre, rstd_pre, pre_ve, pre_rstd, EPS)

            def post(n, half):
                rsqrt(post_ms, n, ms_post, ve_post, rstd_post, post_ve, post_rstd, 4 * EPS if half else EPS)

            for t in range(TT):
                pre(t)
            pool.wait_ge(normed_ready, TT)
            G.dma_start(g_pre, gain(gmpre)).then_inc(g_pre_in, 16)
            for t in range(TT):
                post(t, True)
                pre(TT + t)
            pool.wait_ge(c_ready, 1)
            G.memset(scr[:, 2048:3072], 0.0).then_inc(intra_zeroed, 1)
            for n in range(GLA_H):
                pool.wait_ge(attn_copied, 2 * n + 2)
                for c in range(2):
                    rows = slice(c * CHUNK, (c + 1) * CHUNK)
                    blk = intra[rows, n % 2, :, rows]
                    G.affine_select(out=blk, in_=blk, compare_op=ALU.is_ge, fill=0.0, base=0,
                                    pattern=[[0, TT], [1, CHUNK]], channel_multiplier=-1).then_inc(attn_masked, 1)
            pool.wait_ge(on_ready, GLA_H)
            G.dma_start(g_pre, gain(g2pre)).then_inc(g_pre_in, 16)
            G.dma_start(g_post, gain(gmpost)).then_inc(g_post_in, 16)
            for t in range(TT):
                post(TT + t, False)
                pre(2 * TT + t)
            pool.wait_ge(y_scaled, 2 * TT)
            G.dma_start(g_post, gain(g2post)).then_inc(g_post_in, 16)
            for t in range(TT):
                post(2 * TT + t, True)


_INS = ["x", "ffn1_pre_g", "ffn1_w_gate", "ffn1_w_up", "ffn1_w_down", "ffn1_post_g", "mix_pre_g", "w_in",
        "b_forget", "w_alpha_up", "b_alpha", "gla_norm_g", "w_branch_fox", "w_branch_gla", "w_out",
        "mix_post_g", "ffn2_pre_g", "ffn2_w_gate", "ffn2_w_up", "ffn2_w_down", "ffn2_post_g"]


def kernel(**inputs):
    import numpy as np
    import concourse.bacc as bacc
    from concourse.bass_utils import run_bass_kernel_spmd

    nc = bacc.Bacc("TRN2", target_bir_lowering=False, num_devices=1)
    arrays, args = {}, []
    for name in _INS:
        a = np.ascontiguousarray(inputs[name])[0]
        arrays[f"in_{name}"] = a
        args.append(nc.dram_tensor(f"in_{name}", a.shape, mybir.dt.from_np(a.dtype), kind="ExternalInput").ap())
    out = nc.dram_tensor("out", (N, D), F32, kind="ExternalOutput").ap()
    macaron_layer(nc, *args, out)
    r = run_bass_kernel_spmd(nc, [arrays], core_ids=[0])
    return np.asarray(r.results[0]["out"]).reshape(1, N, D)
```

```python
from contextlib import ExitStack

import concourse.bass as bass
from concourse import mybir

F32 = mybir.dt.float32
F32R = mybir.dt.float32r
ACT = mybir.ActivationFunctionType
ALU = mybir.AluOpType
AX = mybir.AxisListType

P = 128
N = 512
D = 1024
FF = 2816
KD, KF, TT = D // P, FF // P, N // P
HALF = D // 2
UNIT = 1024
SLOTS = 4
EPS = 1e-6

FOX_H, FOX_D = 8, 64
GLA_H, GLA_DK, GLA_DV, CHUNK = 4, 64, 128, 64
RANK, TAU = 16, 16.0
NCH = N // CHUNK
widths = [FOX_H * FOX_D] * 3 + [FOX_H, GLA_H * GLA_DK, GLA_H * GLA_DK, GLA_H * GLA_DV, RANK, GLA_H * GLA_DV, D, D]
(C_FQ, C_FK, C_FV, C_FL, C_GQ, C_GK, C_GV, C_AL, C_GR, C_GF, C_GG) = [sum(widths[:i]) for i in range(11)]
SMALL = 48
ALR = 32

FFN_UNITS = 2 * KF + KF
U_FFN1 = 0
U_MIX = U_FFN1 + FFN_UNITS
(U_SMALL, U_FK, U_FQ, U_FV, U_GV, U_GQ, U_GK, U_GR, U_GATE, U_OUT, U_FFN2) = [
    U_MIX + x for x in (0, 1, 5, 9, 13, 17, 19, 21, 25, 49, 57)]
INPUT = U_GQ - U_MIX
FV_BANKS, GV_BANKS = (1, 2, 3, 4), (0, 5, 6, 7)
B_S, B_PT, B_OT, B_FILL, B_GLA = (1, 2), (3, 7), 0, 4, (5, 6)
U_END = U_FFN2 + FFN_UNITS

CROWS = 96 + FOX_H
MASKED = -1e30
T_Q, T_K, T_V, T_GV, T_GQ, T_GK, T_KST = 0, 4, 8, 12, 16, 18, 20
T_OG = (T_GK, T_GQ, T_GK + 1, T_GQ + 1)
T_GR = (T_Q, T_Q + 1, T_K, T_K + 1)


def slot(u):
    return u % SLOTS


def arrivals(u):
    return 16 * (u // SLOTS + 1)


A_FFN1, A_OUT, A_FFN2 = 0, KF, KF + KD
TILES = 2
PAIRS = 2


def macaron_layer(nc, x, g1pre, w1g, w1u, w1d, g1post, gmpre, w_in, b_forget, w_alpha, b_alpha,
                  gla_g, w_bf, w_bg, w_out, gmpost, g2pre, w2g, w2u, w2d, g2post, out):
    with ExitStack() as ctx:
        def sb(name, shape, dt=F32):
            return ctx.enter_context(nc.sbuf_tensor(name, shape, dt))

        def sem(name):
            return ctx.enter_context(nc.semaphore(name))

        raw = sb("raw", [P, SLOTS, UNIT])
        w_hi = sb("w_hi", [P, SLOTS, UNIT], F32R)
        w_lo = sb("w_lo", [P, SLOTS, UNIT], F32R)
        a_hi = sb("a_hi", [P, SLOTS, N], F32R)
        a_lo = sb("a_lo", [P, SLOTS, N], F32R)
        h = sb("h", [P, TT, D])
        u_hi = sb("u_hi", [P, KD, N], F32R)
        u_lo = sb("u_lo", [P, KD, N], F32R)
        arena = sb("arena", [P, KF, N])
        og_hi = sb("og_hi", [P, GLA_H, N], F32R)
        og_lo = sb("og_lo", [P, GLA_H, N], F32R)
        of_hi, of_lo = a_hi, a_lo
        scr = sb("scr", [P, 7 * 1024])
        silu = scr[:, 0:1024].rearrange("p (b n) -> p b n", b=2)
        scaled = scr[:, 1024:2048]
        junk = scr[:, 2048:3072]
        normed = scr[:, 3072:5120].rearrange("p (b n) -> p b n", b=2)
        g_pre = scr[:, 5120:6144]
        g_post = scr[:, 6144:7168]
        probs = [scr[:, 0:P], scr[:, P:3 * P], scr[:, 6656:6656 + 3 * P], scr[:, 3 * P:7 * P]]
        probsT = scr[:, 1024:2048].rearrange("p (b n) -> p b n", b=2)
        intra = scr[:, 2048:3072].rearrange("p (b t c) -> p b t c", b=2, t=TT)
        state = scr[:, 3072:4096].rearrange("p (n v) -> p n v", n=NCH)
        ga = scr[:, 4096:5120].rearrange("p (j n) -> p j n", j=2)
        gb = scr[:, 5120:6144].rearrange("p (j n) -> p j n", j=2)
        small = scr[:, 6144:6656]
        gr_exp = small
        fsum = scr[:, 6656:7168]
        w_al = scr[:, 6656:6656 + 2 * P]
        msq = scr[:, 4096:6144].rearrange("p (h n) -> p h n", h=GLA_H)
        sig = scr[:, 0:2048].rearrange("p (b n) -> p b n", b=4)
        part = scr[:, 2048:4096].rearrange("p (b n) -> p b n", b=4)
        kst_tok = arena[:, T_KST:T_KST + 2, :].rearrange("p a n -> p (a n)").rearrange("p (t f) -> p t f", t=TT)

        c_parts = sb("c_parts", [CROWS, N], F32R)
        c_neg = sb("c_neg", [CROWS, N], F32R)
        head_sel = sb("head_sel", [CROWS, FOX_H, 2], F32R)
        ident_r = sb("ident_r", [P, P], F32R)
        causal = sb("causal", [P, P], F32R)
        ident = sb("ident", [P, P])
        mean_g = sb("mean_g", [P, P])
        ones = sb("ones", [P, 1])
        half_neg = sb("half_neg", [P, 1])
        eps_t = sb("eps_t", [P, 1])
        bias_small = sb("bias_small", [SMALL, 1])
        bias_alpha = sb("bias_alpha", [P, 2])
        gn = sb("gn", [P, GLA_H])
        ms_post = sb("ms_post", [P, 12])
        ms_pre = sb("ms_pre", [P, 12])
        ve_post = sb("ve_post", [P, 12])
        ve_pre = sb("ve_pre", [P, 12])
        rstd_post = sb("rstd_post", [P, 12])
        rstd_pre = sb("rstd_pre", [P, 12])
        neg_max = sb("neg_max", [P, 32])
        rowsum = sb("rowsum", [P, 32])
        rinv = sb("rinv", [P, 32])
        decay = sb("decay", [P, 2, NCH])

        bank = ctx.enter_context(nc.psum_tensor("bank", [P, 8, HALF], F32))

        raw_in = [sem(f"raw_in{i}") for i in range(SLOTS)]
        x_in = [sem(f"x_in{t}") for t in range(TT)]
        const_in = sem("const_in")
        g_pre_in, g_post_in, w_al_in = sem("g_pre_in"), sem("g_post_in"), sem("w_al_in")
        second_in = [sem("second_in0"), sem("second_in1")]
        hi_ready, lo_ready, unit_used = sem("hi_ready"), sem("lo_ready"), sem("unit_used")
        a_hi_ready, a_lo_ready = sem("a_hi_ready"), sem("a_lo_ready")
        silu_ready, hidden_ready = sem("silu_ready"), sem("hidden_ready")
        y_done, post_ms, post_ve, post_rstd = sem("y_done"), sem("post_ms"), sem("post_ve"), sem("post_rstd")
        y_scaled, h_new = sem("y_scaled"), sem("h_new")
        pre_ms, pre_ve, pre_rstd = sem("pre_ms"), sem("pre_ve"), sem("pre_rstd")
        normed_ready, uT_ready, uT_hi, uT_lo = sem("normed_ready"), sem("uT_ready"), sem("uT_hi"), sem("uT_lo")
        consts, const_step = sem("consts"), sem("const_step")
        evac = sem("evac")
        z_ready, z_out = sem("z_ready"), sem("z_out")
        f_act, f_dve, c_ready, bias_set = sem("f_act"), sem("f_dve"), sem("c_ready"), sem("bias_set")
        a_act, a_dve = sem("a_act"), sem("a_dve")
        scores_ready, max_ready, exp_done = sem("scores_ready"), sem("max_ready"), sem("exp_done")
        rinv_ready, probs_ready, pt_ready, pt_copied, pv_done = (
            sem("rinv_ready"), sem("probs_ready"), sem("pt_ready"), sem("pt_copied"), sem("pv_done"))
        fox_hi, fox_lo, fox_used = sem("fox_hi"), sem("fox_lo"), sem("fox_used")
        kst_ready, kst_copied = sem("kst_ready"), sem("kst_copied")
        attn_ready, attn_copied, attn_masked = sem("attn_ready"), sem("attn_copied"), sem("attn_masked")
        intra_zeroed = sem("intra_zeroed")
        kv_ready, state_ready = sem("kv_ready"), sem("state_ready")
        o_ready, sq_ready, gms_ready, gla_act, on_ready = (
            sem("o_ready"), sem("sq_ready"), sem("gms_ready"), sem("gla_act"), sem("on_ready"))
        ms_out, og_ready = sem("ms_out"), sem("og_ready")
        gr_e, gr_step, gr_ready = sem("gr_e"), sem("gr_step"), sem("gr_ready")
        og_raw, og_hi_ready = sem("og_raw"), sem("og_hi_ready")
        og_lo_ready, merged = sem("og_lo_ready"), sem("merged")
        gate_sig, gate_mul = sem("gate_sig"), sem("gate_mul")
        out_done = sem("out_done")

        steps = [(hh, qb) for hh in range(FOX_H) for qb in range(TT)]
        NS = len(steps)
        gla_steps = [("kst", 0), ("kst", 1)]
        for j in range(2):
            gla_steps += [("attn", 2 * j), ("attn", 2 * j + 1), ("kv", 2 * j), ("kv", 2 * j + 1),
                          ("o", 2 * j), ("ms", 2 * j), ("o", 2 * j + 1), ("ms", 2 * j + 1)]

        cum = scr[:, 2048:2560]

        def feature_bank(u):
            for first, banks in ((U_FK, (1, 2, 3, 4)), (U_FQ, (5, 6, 7, 0))):
                if first <= u < first + len(banks):
                    return banks[u - first]

        def y_tile(t):
            return bank[:, 2 * t:2 * t + 2, :]

        def uT_psum(t):
            return bank[:, 2 * t:2 * t + 2, :].rearrange("p b (k n) -> p (b k) n", k=KD // 2)

        def gain(g):
            return g.rearrange("(o n) -> o n", o=1).to_broadcast([P, D])

        gla_slots = {17: (0, 1), 18: (2, 3), 19: (4, 5), 22: (6,), 23: (7, 8), 24: (9, 10), 25: (11, 12),
                     26: (13,), 29: (14,), 30: (15,), 31: (16,), 32: (17,)}
        gated_slots = {25: 0, 26: 1, 31: 2, 35: 3}
        SLOTS_B = NS + 4
        FILL = {}
        for f in range(8):
            k = 0
            for n, count in enumerate((3, 3, 2) if f < 7 else (1, 1, 1, 1, 2, 2)):
                FILL[4 * f + n] = (f, range(k, k + count))
                k += count
        FILLED = {4 * f + 3 if f < 7 else 34: f for f in range(8)}
        silu_slots = {SLOTS_B - 1: ((GLA_H - 1, 0), (GLA_H - 1, 1))}
        for n in range(GLA_H - 1):
            for piece in range(2):
                silu_slots[4 * (n + 4) + 4 + piece] = ((n, piece),)

        def gbank(g):
            return bank[:, B_GLA[g % 2], :]

        plain = {}
        for first, count, col in ((U_FK, 4, C_FK), (U_FQ, 4, C_FQ), (U_GQ, 2, C_GQ), (U_GK, 2, C_GK), (U_GR, 4, C_GR)):
            for m in range(count):
                plain[first + m] = col + m * P

        def kmajor(w, cols):
            return w[:, cols].rearrange("(k p) c -> p k c", p=P)

        block = ctx.enter_context(nc.Block())

        @block.sync
        def _(sp):
            def free(u, i=0):
                sp.wait_ge(lo_ready, i + (u - SLOTS + 1))

            def load(u, src, dst=None, i=0):
                free(u, i)
                dst = raw[:, slot(u), :] if dst is None else dst
                sp.dma_start(dst, src).then_inc(raw_in[slot(u)], 16)

            def tiles(u):
                return raw[:, slot(u), :].rearrange("p (k c) -> p k c", k=KD)

            def first_load(j):
                f = j // 2 * P
                sp.dma_start(tiles(j), kmajor((w1g, w1u)[j % 2], slice(f, f + P))).then_inc(raw_in[slot(j)], 16)

            def ffn_loads(u0, wg, wu, wd, peel):
                with sp.Fori(peel // 4, KF // 2) as i:
                    for j in range(4):
                        w = (wg, wu)[j % 2]
                        load(u0 + j, kmajor(w, bass.ds(i * 2 * P + (j // 2) * P, P)), tiles(u0 + j), i * 4)
                with sp.Fori(0, KF // 4) as i:
                    for j in range(4):
                        load(u0 + 2 * KF + j, wd[bass.ds(i * 4 * P + j * P, P), :], None, i * 4)
                for k in range(KF // 4 * 4, KF):
                    load(u0 + 2 * KF + k, wd[k * P:(k + 1) * P, :])

            for t in range(TT):
                sp.dma_start(h[:, t, :], x[t * P:(t + 1) * P, :]).then_inc(x_in[t], 16)
                if t:
                    first_load(t - 1)
            first_load(TT - 1)
            ffn_loads(U_FFN1, w1g, w1u, w1d, SLOTS)

            free(U_SMALL)
            st = raw[:, slot(U_SMALL), 0:KD * SMALL].rearrange("p (k c) -> p k c", k=KD)
            sp.dma_start(st[:, :, 0:FOX_H], kmajor(w_in, slice(C_FL, C_FL + FOX_H))).then_inc(raw_in[slot(U_SMALL)], 16)
            sp.dma_start(st[:, :, ALR:ALR + RANK], kmajor(w_in, slice(C_AL, C_AL + RANK))).then_inc(second_in[0], 16)
            for u in range(U_FK, U_GATE):
                if u == U_FK + 3:
                    sp.wait_ge(y_scaled, TT)
                    sp.dma_start(w_al[ALR:ALR + RANK, :], w_alpha).then_inc(w_al_in, 16)
                if u in plain:
                    load(u, kmajor(w_in, slice(plain[u], plain[u] + P)), tiles(u))
                else:
                    first, col = (U_FV, C_FV) if u < U_GV else (U_GV, C_GV)
                    k = 2 * (u - first)
                    load(u, w_in[k * P:(k + 2) * P, col:col + N].rearrange("(k p) c -> p k c", p=P),
                         raw[:, slot(u), :].rearrange("p (k c) -> p k c", k=2))
            with sp.Fori(0, KD // 4) as i:
                for m in range(4):
                    u = U_GATE + 3 * m
                    col = i * 4 * P + m * P
                    load(u, kmajor(w_in, bass.ds(col + C_GF, P)), tiles(u), i * 12)
                    load(u + 1, kmajor(w_in, bass.ds(col + C_GG, P)), tiles(u + 1), i * 12)
                    free(u + 2, i * 12)
                    sp.nop(nofuse=True)
                    sp.dma_start(tiles(u + 2)[:, 0:4, :], kmajor(w_bf, bass.ds(col, P))).then_inc(raw_in[slot(u + 2)], 16)
                    sp.dma_start(tiles(u + 2)[:, 4:8, :], kmajor(w_bg, bass.ds(col, P))).then_inc(second_in[m % 2], 16)
            for k in range(KD):
                if k == 2:
                    free(U_OUT + k)
                    for c, arrived in ((0, raw_in[slot(U_OUT + k)]), (HALF, second_in[0])):
                        sp.dma_start(raw[:, slot(U_OUT + k), c:c + HALF],
                                     w_out[k * P:(k + 1) * P, c:c + HALF]).then_inc(arrived, 16)
                else:
                    load(U_OUT + k, w_out[k * P:(k + 1) * P, :])
            ffn_loads(U_FFN2, w2g, w2u, w2d, 0)
            for t in range(TT):
                sp.wait_ge(h_new, 8 + t + 1)
                sp.dma_start(out[t * P:(t + 1) * P, :], h[:, t, :]).then_inc(out_done, 16)
            sp.wait_ge(out_done, 16 * TT)

        @block.scalar
        def _(act):
            consts_dma = [(bias_small[0:FOX_H, :], b_forget.rearrange("(h o) -> h o", o=1)),
                          (bias_alpha[:, :], b_alpha.rearrange("(j p) -> p j", p=P)),
                          (gn[:, :], gla_g.rearrange("(h p) -> p h", p=P))]
            act.wait_ge(bias_set, 1)
            for dst, src in consts_dma:
                act.dma_start(dst, src, allow_slow_non_contiguous=True).then_inc(const_in, 16)

            def split(u, i=0, per=0, second=None):
                act.wait_ge(raw_in[slot(u)], i * (16 * per // SLOTS) + arrivals(u))
                if second is not None:
                    act.wait_ge(*second)
                if not isinstance(i, int) or u + per * i >= SLOTS:
                    act.wait_ge(unit_used, i * per + (u - SLOTS + 1))
                nc.scalar.activation(w_hi[:, slot(u), :], raw[:, slot(u), :], ACT.Copy).then_inc(hi_ready, 1)

            def split_a(u, tile):
                nc.scalar.activation(a_hi[:, slot(u), :], tile, ACT.Copy).then_inc(a_hi_ready, 1)

            squared = []

            def junk_free(mine, count):
                for last in squared:
                    act.wait_ge(*last)
                squared[:] = [(mine, count)]

            def pre_sq(q, t):
                if q < TT:
                    act.wait_ge(x_in[t], 16)
                else:
                    act.wait_ge(h_new, q - TT + 1)
                junk_free(pre_ms, q + 1)
                nc.scalar.activation(junk, h[:, t, :], ACT.Square, scale=D ** -0.5,
                                     accum_out=ms_pre[:, q:q + 1]).then_inc(pre_ms, 1)

            def post_sq(r, t, half):
                if t < TT - 1:
                    act.wait_ge(y_done, (TT - 1) * (r // TT) + t + 1)
                else:
                    act.wait_ge(unit_used, (U_MIX, U_FFN2, U_END)[r // TT])
                junk_free(post_ms, r + 1)
                nc.scalar.activation(junk, y_tile(t), ACT.Square, scale=(2 if half else 1) * D ** -0.5,
                                     accum_out=ms_post[:, r:r + 1]).then_inc(post_ms, 1)

            def uT_evac(q, t):
                act.wait_ge(uT_ready, q + 1)
                nc.scalar.activation(u_hi[:, :, t * P:(t + 1) * P], uT_psum(t), ACT.Copy).then_inc(uT_hi, 1)

            def boundary(b, u_next, small_next=False):
                r, q, half = TT * (b - 1), TT * b, b != 2
                if b == 3:
                    for t in range(TT):
                        post_sq(r + t, t, half)
                    return
                for t in range(2):
                    post_sq(r + t, t, half)
                    pre_sq(q + t, t)
                post_sq(r + 2, 2, half)
                uT_evac(q, 0)
                split(u_next, second=(second_in[0], 16) if small_next else None)
                uT_evac(q + 1, 1)
                post_sq(r + 3, 3, half)
                split(u_next + 1)
                pre_sq(q + 2, 2)
                split(u_next + 2)
                split(u_next + 3)
                pre_sq(q + 3, 3)
                uT_evac(q + 2, 2)
                uT_evac(q + 3, 3)

            def ffn(u0, layer, a0):
                def pair(i, down):
                    for j in range(4):
                        if j % 2 == 0:
                            act.wait_ge(unit_used, i * 4 + (u0 + j + 1))
                            nc.scalar.activation(silu[:, j // 2, :], bank[:, j, :], ACT.Silu).then_inc(silu_ready, 1)
                        split(u0 + j + 4, i, 4)
                        if down:
                            split_a(u0 + j + 4, arena[:, j, :])

                with act.Fori(0, KF // 2 - 1) as i:
                    pair(i, False)
                act.wait_ge(hidden_ready, PAIRS + layer * KF + 4)
                pair(KF // 2 - 1, True)
                ud = u0 + 2 * KF
                with act.Fori(0, 4) as i:
                    for j in range(4):
                        split(ud + j + 4, i, 4)
                        act.wait_ge(hidden_ready, i * 4 + (PAIRS + layer * KF + j + 5))
                        split_a(ud + j + 4, arena[:, bass.ds(i * 4 + (j + 4), 1), :])
                for k in (20, 21):
                    split(ud + k)
                    act.wait_ge(hidden_ready, PAIRS + layer * KF + k + 1)
                    split_a(ud + k, arena[:, k, :])

            pre_sq(0, 0)
            pre_sq(1, 1)
            uT_evac(0, 0)
            split(0)
            uT_evac(1, 1)
            pre_sq(2, 2)
            split(1)
            pre_sq(3, 3)
            split(2)
            split(3)
            uT_evac(2, 2)
            uT_evac(3, 3)
            ffn(U_FFN1, 0, A_FFN1)
            boundary(1, U_MIX, small_next=True)

            act.wait_ge(const_in, 16 * len(consts_dma))
            for s in range(INPUT):
                v = U_MIX + s
                act.wait_ge(unit_used, v + 1)
                if s == 0:
                    nc.scalar.activation(small[0:SMALL, :], bank[0:SMALL, 0, :], ACT.Identity,
                                         bias=bias_small[:, :]).then_inc(evac, 1)
                elif v in plain:
                    tile = T_K + v - U_FK if v < U_FQ else T_Q + v - U_FQ
                    nc.scalar.activation(arena[:, tile, :], bank[:, feature_bank(v), :], ACT.Copy,
                                         scale=1.0 if v < U_FQ else FOX_D ** -0.5).then_inc(evac, 1)
                elif v in (U_FV + 3, U_GV + 3):
                    for t in range(TT):
                        tile, banks = (T_V, FV_BANKS) if v < U_GV else (T_GV, GV_BANKS)
                        nc.scalar.activation(arena[:, tile + t, :], bank[:, banks[t], :],
                                             ACT.Copy).then_inc(evac, 1)
                if s == 1:
                    act.wait_ge(evac, 1)
                    nc.scalar.activation(fsum[0:FOX_H, :], small[0:FOX_H, :], ACT.Abs).then_inc(f_act, 1)
                    act.wait_ge(f_act, 1)
                    nc.scalar.activation(fsum[0:FOX_H, :], fsum[0:FOX_H, :], ACT.Exp, scale=-1.0).then_inc(f_act, 1)
                    act.wait_ge(f_act, 2)
                    nc.scalar.activation(fsum[0:FOX_H, :], fsum[0:FOX_H, :], ACT.Ln, bias=1.0).then_inc(f_act, 1)
                if s == 3:
                    for j in range(2):
                        act.wait_ge(z_ready, j + 1)
                        nc.scalar.activation(ga[:, j, :], bank[:, 6 + j, :], ACT.Identity,
                                             bias=bias_alpha[:, j:j + 1]).then_inc(z_out, 1)
                if s == 4:
                    act.wait_ge(z_out, 2)
                    nc.scalar.activation(gb, ga, ACT.Abs).then_inc(a_act, 1)
                    act.wait_ge(a_act, 1)
                    nc.scalar.activation(gb, gb, ACT.Exp, scale=-1.0).then_inc(a_act, 1)
                    act.wait_ge(a_act, 2)
                    nc.scalar.activation(gb, gb, ACT.Ln, bias=1.0).then_inc(a_act, 1)
                if s == 5:
                    act.wait_ge(a_dve, 2)
                    nc.scalar.activation(ga, gb, ACT.Exp, scale=1.0 / TAU).then_inc(a_act, 1)
                if s == 6:
                    act.wait_ge(a_dve, 3)
                    kst = arena[:, T_KST:T_KST + 2, :]
                    nc.scalar.activation(kst, kst, ACT.Exp, scale=1.0 / TAU).then_inc(a_act, 1)
                split(v + 4)

            for sl in range(SLOTS_B):
                if sl in FILLED:
                    f = FILLED[sl]
                    v = U_GQ + f
                    tile, scale = ((T_GQ + f, GLA_DK ** -0.5) if v < U_GK else (T_GK + v - U_GK, 1.0) if v < U_GR
                                   else (T_GR[v - U_GR], 1.0))
                    act.wait_ge(unit_used, v + 1)
                    if v >= U_GR:
                        act.wait_ge(scores_ready, 16)
                    nc.scalar.activation(arena[:, tile, :], bank[:, B_FILL, :], ACT.Copy, scale=scale).then_inc(evac, 1)
                if sl < NS:
                    hh, qb = steps[sl]
                    kend = (qb + 1) * P
                    act.wait_ge(max_ready, sl + 1)
                    if sl >= TT:
                        act.wait_ge(pt_ready, sl - TT + 1)
                    nc.scalar.activation(probs[qb], bank[:, B_S[sl % 2], 0:kend], ACT.Exp,
                                         bias=neg_max[:, sl:sl + 1],
                                         accum_out=rowsum[:, sl:sl + 1]).then_inc(exp_done, 1)
                if 2 <= sl < NS + 2:
                    s = sl - 2
                    kend = (steps[s][1] + 1) * P
                    act.wait_ge(pt_ready, s + 1)
                    if s >= 2:
                        act.wait_ge(pv_done, s - 1)
                    nc.scalar.activation(probsT[:, s % 2, 0:kend], bank[:, B_PT[s % 2], 0:kend],
                                         ACT.Copy).then_inc(pt_copied, 1)
                if sl >= 10 and (sl - 10) % 8 == 0:
                    p = (sl - 10) // 8
                    act.wait_ge(pv_done, 8 * p + 8)
                    nc.scalar.activation(of_hi[:, p, :], bank[:, B_OT, :], ACT.Copy).then_inc(fox_hi, 1)
                if sl == 9:
                    act.wait_ge(a_dve, 5)
                    nc.scalar.activation(ga, gb, ACT.Exp, scale=-1.0 / TAU).then_inc(a_act, 1)
                if sl in FILLED:
                    if v >= U_GR:
                        act.wait_ge(evac, 18 + f)
                        if v > U_GR:
                            act.wait_ge(gr_ready, v - U_GR)
                        nc.scalar.activation(gr_exp, arena[:, tile, :], ACT.Exp, scale=-1.0).then_inc(gr_e, 1)
                    split(v + 4, second=(second_in[0], 32) if v + 4 == U_GATE + 2 else None)
                for g in gla_slots.get(sl, ()):
                    kind, n = gla_steps[g]
                    if kind == "kst" and n == 1:
                        act.wait_ge(kst_ready, 2)
                        for i in range(2):
                            nc.scalar.activation(kst_tok[:, 2 * i:2 * i + 2, :].rearrange("p t f -> p (t f)"),
                                                 gbank(i), ACT.Copy).then_inc(kst_copied, 1)
                    if kind == "attn":
                        act.wait_ge(attn_ready, n + 1)
                        act.wait_ge(intra_zeroed, 1)
                        if n >= 2:
                            act.wait_ge(o_ready, n - 1)
                        src = gbank(g).rearrange("p (t c) -> p t c", t=TT)
                        for c in range(2):
                            rows = slice(c * CHUNK, (c + 1) * CHUNK)
                            nc.scalar.activation(intra[rows, n % 2, :, rows], src[rows, :, rows], ACT.Copy).then_inc(attn_copied, 1)
                    if kind == "o":
                        act.wait_ge(o_ready, n + 1)
                        nc.scalar.activation(msq[:, n, :], gbank(g), ACT.Square).then_inc(sq_ready, 1)
                    if kind == "ms":
                        act.wait_ge(gms_ready, n + 1)
                        nc.scalar.activation(msq[:, n, :], gbank(g), ACT.Copy).then_inc(ms_out, 1)
                if sl == NS + 2:
                    act.wait_ge(ms_out, GLA_H)
                    nc.scalar.activation(msq, msq, ACT.Ln, bias=eps_t[:, :]).then_inc(gla_act, 1)
                    act.wait_ge(gla_act, 1)
                    nc.scalar.activation(msq, msq, ACT.Exp, scale=-0.5).then_inc(gla_act, 1)
            for n in range(GLA_H):
                act.wait_ge(og_ready, n + 1)
                nc.scalar.activation(og_hi[:, n, :], arena[:, T_OG[n], :], ACT.Copy).then_inc(og_hi_ready, 1)

            act.wait_ge(pv_done, NS)
            def four_tiles(i, last):
                for m in range(4):
                    for j in range(3):
                        v = U_GATE + 3 * m + j
                        if j < 2:
                            act.wait_ge(unit_used, i * 12 + (v + 1))
                            nc.scalar.activation(sig[:, 2 * (m % 2) + j, :], bank[:, 4 * ((m + 1) % 2) + j, :],
                                                 ACT.Sigmoid).then_inc(gate_sig, 1)
                        elif last and m == 3:
                            act.wait_ge(fox_used, KD)
                            for k in range(4):
                                act.wait_ge(merged, TILES + k + 1)
                                split_a(U_OUT + k, arena[:, k, :])
                        k = 3 * m + j + 4
                        mm = k // 3
                        second = (second_in[mm % 2], i * 32 + 16 * (mm // 2 + 1 + (mm + 1) % 2)) if k % 3 == 2 else None
                        split(v + 4, i, 12, second)

            with act.Fori(0, KD // 4 - 1) as i:
                four_tiles(i, False)
            four_tiles(KD // 4 - 1, True)

            act.wait_ge(merged, TILES + KD)
            for k in range(4, KD):
                split(U_OUT + k)
                split_a(U_OUT + k, arena[:, k, :])
            boundary(2, U_FFN2)
            ffn(U_FFN2, 1, A_FFN2)
            boundary(3, None)

        @block.vector
        def _(dve):
            V = nc.vector

            def split(u, i=0, per=0):
                dve.wait_ge(hi_ready, i * per + (u + 1))
                V.tensor_tensor(w_lo[:, slot(u), :], raw[:, slot(u), :], w_hi[:, slot(u), :].bitcast(F32),
                                ALU.subtract).then_inc(lo_ready, 1)

            def split_a(a, u, tile, i=0):
                dve.wait_ge(a_hi_ready, i * 4 + (a + 1))
                V.tensor_tensor(a_lo[:, slot(u), :], tile, a_hi[:, slot(u), :].bitcast(F32),
                                ALU.subtract).then_inc(a_lo_ready, 1)

            def norm_in(q, t):
                dve.wait_ge(pre_rstd, q + 1)
                if t == 0:
                    dve.wait_ge(g_pre_in, 16 * (q // TT + 1))
                if q >= TT:
                    dve.wait_ge(h_new, q - TT + 1)
                if q >= 2:
                    dve.wait_ge(uT_ready, q - 1)
                V.scalar_tensor_tensor(normed[:, q % 2, :], h[:, t, :], rstd_pre[:, q:q + 1], g_pre,
                                       ALU.mult, ALU.mult).then_inc(normed_ready, 1)

            def uT_rest(q, t):
                dve.wait_ge(uT_hi, q + 1)
                cols = slice(t * P, (t + 1) * P)
                V.tensor_tensor(u_lo[:, :, cols], uT_psum(t), u_hi[:, :, cols].bitcast(F32),
                                ALU.subtract).then_inc(uT_lo, 1)

            def with_gain(r, t):
                dve.wait_ge(post_ms, r + 1)
                if t == 0:
                    dve.wait_ge(g_post_in, 16 * (r // TT + 1))
                if r >= 1:
                    dve.wait_ge(h_new, r)
                V.tensor_tensor(scaled, y_tile(t), g_post.rearrange("p (b n) -> p b n", b=2), ALU.mult).then_inc(y_scaled, 1)

            def add(r, t):
                dve.wait_ge(y_scaled, r + 1)
                dve.wait_ge(post_rstd, r + 1)
                V.scalar_tensor_tensor(h[:, t, :], scaled, rstd_post[:, r:r + 1], h[:, t, :],
                                       ALU.mult, ALU.add).then_inc(h_new, 1)

            def boundary(b, u_next):
                r, q = TT * (b - 1), TT * b
                if b == 3:
                    for t in range(TT):
                        with_gain(r + t, t)
                        add(r + t, t)
                    return
                for t in range(2):
                    with_gain(r + t, t)
                    add(r + t, t)
                    norm_in(q + t, t)
                uT_rest(q, 0)
                split(u_next)
                with_gain(r + 2, 2)
                uT_rest(q + 1, 1)
                add(r + 2, 2)
                with_gain(r + 3, 3)
                split(u_next + 1)
                norm_in(q + 2, 2)
                add(r + 3, 3)
                dve.wait_ge(lo_ready, u_next + 3)
                split(u_next + 3)
                norm_in(q + 3, 3)
                uT_rest(q + 2, 2)
                uT_rest(q + 3, 3)

            def ffn(u0, layer, a0):
                def pair(i, down):
                    for j in range(4):
                        if j % 2:
                            dve.wait_ge(unit_used, i * 4 + (u0 + j + 1))
                            dve.wait_ge(silu_ready, i * 2 + (layer * KF + j // 2 + 1))
                            f = (bass.ds(i * 2 + j // 2, 1))
                            V.tensor_tensor(arena[:, f, :], silu[:, j // 2, :].rearrange("p (o n) -> p o n", o=1),
                                            bank[:, j:j + 1, :], ALU.mult).then_inc(hidden_ready, 1)
                        split(u0 + j + 4, i, 4)
                        if down:
                            split_a(a0 + j, u0 + j + 4, arena[:, j, :])

                with dve.Fori(0, KF // 2 - 1) as i:
                    pair(i, False)
                dve.wait_ge(hidden_ready, PAIRS + layer * KF + 4)
                pair(KF // 2 - 1, True)
                ud = u0 + 2 * KF
                with dve.Fori(0, 4) as i:
                    for j in range(4):
                        split(ud + j + 4, i, 4)
                        dve.wait_ge(hidden_ready, i * 4 + (PAIRS + layer * KF + j + 5))
                        split_a(a0 + j + 4, ud + j + 4, arena[:, bass.ds(i * 4 + (j + 4), 1), :].rearrange("p o n -> p (o n)"), i)
                for k in (20, 21):
                    split(ud + k)
                    dve.wait_ge(hidden_ready, PAIRS + layer * KF + k + 1)
                    split_a(a0 + k, ud + k, arena[:, k, :])

            V.memset(bias_small[:, :], 0.0).then_inc(bias_set, 1)
            V.memset(ones[:, :], 1.0)
            V.memset(eps_t[:, :], EPS).then_inc(merged, TILES)
            V.memset(c_parts[:, :].bitcast(F32), 0.0)
            V.memset(mean_g[:, :], 1.0 / GLA_DV).then_inc(hidden_ready, PAIRS)
            dve.wait_ge(const_step, 10)
            V.tensor_copy(ident_r[:, :], ident[:, :])
            V.tensor_copy(causal[:, :], arena[:, 0, 0:P])
            V.tensor_copy(head_sel[:, :, :].rearrange("p h o -> p (h o)"), arena[0:CROWS, 1, 0:2 * FOX_H]).then_inc(consts, 1)

            norm_in(0, 0)
            norm_in(1, 1)
            uT_rest(0, 0)
            split(0)
            uT_rest(1, 1)
            norm_in(2, 2)
            split(1)
            norm_in(3, 3)
            split(2)
            split(3)
            uT_rest(2, 2)
            uT_rest(3, 3)
            ffn(U_FFN1, 0, A_FFN1)
            boundary(1, U_MIX)

            for s in range(INPUT):
                v = U_MIX + s
                if s == 1:
                    dve.wait_ge(f_act, 3)
                    V.scalar_tensor_tensor(fsum[0:FOX_H, :], small[0:FOX_H, :], 0.0, fsum[0:FOX_H, :],
                                           ALU.min, ALU.subtract).then_inc(f_dve, 1)
                    dve.wait_ge(f_dve, 1)
                    V.tensor_tensor_scan(cum[0:FOX_H, :], ones[0:FOX_H, 0:1].to_broadcast([FOX_H, N]), fsum[0:FOX_H, :],
                                         0.0, ALU.mult, ALU.add).then_inc(f_dve, 1)
                    dve.wait_ge(f_dve, 2)
                    for r in (0, 64):
                        last = V.tensor_copy(c_parts[r:r + FOX_H, :], cum[0:FOX_H, :])
                    last.then_inc(f_dve, 1)
                    dve.wait_ge(f_dve, 3)
                    for r in (32, 96):
                        last = V.tensor_tensor(c_parts[r:r + FOX_H, :], cum[0:FOX_H, :], c_parts[0:FOX_H, :].bitcast(F32),
                                               ALU.subtract)
                    last.then_inc(f_dve, 1)
                    dve.wait_ge(f_dve, 4)
                    V.tensor_scalar(c_neg[:, :], c_parts[:, :].bitcast(F32), -1.0, None, ALU.mult).then_inc(c_ready, 1)
                if s == 4:
                    dve.wait_ge(a_act, 3)
                    V.scalar_tensor_tensor(ga, ga, 0.0, gb, ALU.min, ALU.subtract).then_inc(a_dve, 1)
                    dve.wait_ge(a_dve, 1)
                    for j in range(2):
                        for n in range(NCH):
                            cols = slice(n * CHUNK, (n + 1) * CHUNK)
                            last = V.tensor_tensor_scan(gb[:, j, cols], ones[:, 0:1].to_broadcast([P, CHUNK]), ga[:, j, cols],
                                                        0.0, ALU.mult, ALU.add)
                    last.then_inc(a_dve, 1)
                if s == 5:
                    dve.wait_ge(a_dve, 2)
                    for j in range(2):
                        bj = gb[:, j, :].rearrange("p (n c) -> p n c", n=NCH)
                        last = V.tensor_tensor(arena[:, T_KST + j, :].rearrange("p (n c) -> p n c", n=NCH),
                                               bj[:, :, CHUNK - 1:CHUNK].to_broadcast([P, NCH, CHUNK]), bj, ALU.subtract)
                    last.then_inc(a_dve, 1)
                    dve.wait_ge(a_act, 4)
                    ends = ga.rearrange("p j (n c) -> p j n c", n=NCH)[:, :, :, CHUNK - 1]
                    V.tensor_copy(decay[:, :, :], ends).then_inc(a_dve, 1)
                split(v + 4)

            for sl in range(SLOTS_B):
                if sl < NS:
                    kend = (steps[sl][1] + 1) * P
                    dve.wait_ge(scores_ready, sl + 1)
                    V.tensor_reduce(neg_max[:, sl:sl + 1], bank[:, B_S[sl % 2], 0:kend], AX.X, ALU.max,
                                    negate=True).then_inc(max_ready, 1)
                if 1 <= sl <= NS:
                    s = sl - 1
                    dve.wait_ge(exp_done, s + 1)
                    V.reciprocal(rinv[:, s:s + 1], rowsum[:, s:s + 1]).then_inc(rinv_ready, 1)
                    dve.wait_ge(rinv_ready, s + 1)
                    V.tensor_scalar(probs[steps[s][1]], probs[steps[s][1]], rinv[:, s:s + 1], None,
                                    ALU.mult).then_inc(probs_ready, 1)
                for g in gla_slots.get(sl - 1, ()):
                    kind, n = gla_steps[g]
                    if kind == "kv" and n % 2:
                        j = n // 2
                        dve.wait_ge(kv_ready, n + 1)
                        if j:
                            dve.wait_ge(o_ready, 2)
                        for c in range(NCH - 1):
                            kv = gbank(g - 1 + c % 2)[:, (c // 2) * GLA_DV:(c // 2 + 1) * GLA_DV]
                            if c == 0:
                                V.tensor_copy(state[:, 1, :], kv).then_inc(state_ready, 1)
                            else:
                                dve.wait_ge(state_ready, j * (NCH - 1) + c)
                                V.scalar_tensor_tensor(state[:, c + 1, :], state[:, c, :], decay[:, j, c:c + 1],
                                                       kv, ALU.mult, ALU.add).then_inc(state_ready, 1)
                if sl >= 10 and (sl - 10) % 8 == 0:
                    p = (sl - 10) // 8
                    dve.wait_ge(fox_hi, p + 1)
                    V.tensor_tensor(of_lo[:, p, :], bank[:, B_OT, :], of_hi[:, p, :].bitcast(F32),
                                    ALU.subtract).then_inc(fox_lo, 1)
                if sl == 8:
                    dve.wait_ge(evac, 19)
                    qin = arena[:, T_GQ:T_GQ + 2, :]
                    V.tensor_tensor(qin, qin, ga, ALU.mult).then_inc(a_dve, 1)
                if sl == 16:
                    dve.wait_ge(evac, 21)
                    dve.wait_ge(a_act, 6)
                    kin, kst = arena[:, T_GK:T_GK + 2, :], arena[:, T_KST:T_KST + 2, :]
                    V.tensor_tensor(kst, kst, kin, ALU.mult).then_inc(a_dve, 1)
                    V.tensor_tensor(kin, kin, ga, ALU.mult).then_inc(a_dve, 1)
                if sl in FILLED:
                    split(U_GQ + FILLED[sl] + 4)
                for n, piece in silu_slots.get(sl, ()):
                    if piece == 0:
                        dve.wait_ge(gr_e, n + 1)
                        V.tensor_scalar(gr_exp, gr_exp, 1.0, None, ALU.add).then_inc(gr_step, 1)
                        dve.wait_ge(gr_step, 3 * n + 1)
                    cols = slice(piece * N // 2, (piece + 1) * N // 2)
                    V.reciprocal(gr_exp[:, cols], gr_exp[:, cols]).then_inc(gr_step, 1)
                    if piece == 1:
                        dve.wait_ge(gr_step, 3 * n + 3)
                        gr = arena[:, T_GR[n], :]
                        V.tensor_tensor(gr, gr, gr_exp, ALU.mult).then_inc(gr_ready, 1)
                if sl in gated_slots:
                    n = gated_slots[sl]
                    dve.wait_ge(gr_ready, n + 1)
                    dve.wait_ge(on_ready, n + 1)
                    tile = arena[:, T_OG[n], :]
                    V.tensor_tensor(tile, tile, arena[:, T_GR[n], :], ALU.mult).then_inc(og_raw, 1)
                for g in gla_slots.get(sl, ()):
                    kind, n = gla_steps[g]
                    if kind == "o":
                        dve.wait_ge(sq_ready, n + 1)
                        V.tensor_scalar(arena[:, T_OG[n], :], gbank(g), gn[:, n:n + 1], None, ALU.mult).then_inc(on_ready, 1)
            for n in range(GLA_H + 1):
                if n < GLA_H:
                    tile = arena[:, T_OG[n], :]
                    dve.wait_ge(og_raw, n + 1)
                    dve.wait_ge(gla_act, 2)
                    V.tensor_tensor(tile, tile, msq[:, n, :], ALU.mult).then_inc(og_ready, 1)
                if n:
                    dve.wait_ge(og_hi_ready, n)
                    V.tensor_tensor(og_lo[:, n - 1, :], arena[:, T_OG[n - 1], :], og_hi[:, n - 1, :].bitcast(F32),
                                    ALU.subtract).then_inc(og_lo_ready, 1)

            def four_tiles(i, last):
                for m in range(4):
                    b0, s0 = 4 * ((m + 1) % 2), 2 * (m % 2)
                    v = U_GATE + 3 * m
                    split(v + 4, i, 12)
                    split(v + 5, i, 12)
                    if last and m == 3:
                        dve.wait_ge(fox_used, KD)
                        for k in range(4):
                            dve.wait_ge(merged, TILES + k + 1)
                            split_a(A_OUT + k, U_OUT + k, arena[:, k, :])
                    dve.wait_ge(gate_sig, i * 8 + (2 * m + 2))
                    dve.wait_ge(unit_used, i * 12 + (v + 3))
                    V.tensor_tensor(part[:, s0:s0 + 2, :], sig[:, s0:s0 + 2, :], bank[:, b0 + 2:b0 + 4, :],
                                    ALU.mult).then_inc(gate_mul, 1)
                    dve.wait_ge(gate_mul, i * 4 + (m + 1))
                    V.tensor_tensor(arena[:, bass.ds(i * 4 + m, 1), :], part[:, s0:s0 + 1, :], part[:, s0 + 1:s0 + 2, :],
                                    ALU.add).then_inc(merged, 1)
                    split(v + 6, i, 12)

            with dve.Fori(0, KD // 4 - 1) as i:
                four_tiles(i, False)
            four_tiles(KD // 4 - 1, True)

            dve.wait_ge(merged, TILES + KD)
            for k in range(4, KD):
                split(U_OUT + k)
                split_a(A_OUT + k, U_OUT + k, arena[:, k, :])
            boundary(2, U_FFN2)
            ffn(U_FFN2, 1, A_FFN2)
            boundary(3, None)

        @block.tensor
        def _(pe):
            mm = nc.tensor.matmul

            def weights(u, i=0, per=0):
                pe.wait_ge(lo_ready, i * per + (u + 1))

            def feature_product(u, dst, k_tiles=range(KD), rhs_hi=u_hi, rhs_lo=u_lo, k0=0, k1=KD - 1):
                for k in k_tiles:
                    w = slice(k * P, (k + 1) * P)
                    mm(dst, w_hi[:, slot(u), w], rhs_hi[:, k - k0, :], start=k == k0, stop=False)
                    mm(dst, w_hi[:, slot(u), w], rhs_lo[:, k - k0, :], start=False, stop=False)
                    last = mm(dst, w_lo[:, slot(u), w], rhs_hi[:, k - k0, :], start=False, stop=k == k1)
                return last

            def token_product(u, t, first, final):
                s, toks = slot(u), slice(t * P, (t + 1) * P)
                for a, w in ((a_hi, w_hi), (a_hi, w_lo), (a_lo, w_hi)):
                    for c in range(2):
                        last = mm(bank[:, 2 * t + c, :], a[:, s, toks], w[:, s, c * HALF:(c + 1) * HALF],
                                  start=first and a is a_hi and w is w_hi, stop=final and a is a_lo)
                return last

            def transposes(q, t):
                pe.wait_ge(normed_ready, q + 1)
                for k in range(KD):
                    last = nc.tensor.transpose(bank[:, 2 * t + k // 4, (k % 4) * P:(k % 4 + 1) * P],
                                               normed[:, q % 2, k * P:(k + 1) * P], ident[:, :])
                last.then_inc(uT_ready, 1)

            def last_units(b, u0, a0):
                q = TT * b
                for t in range(TT):
                    for k in range(4):
                        if t == 0:
                            weights(u0 + k)
                            pe.wait_ge(a_lo_ready, a0 + k + 1)
                        last = token_product(u0 + k, t, False, k == 3)
                        if t == TT - 1:
                            last.then_inc(unit_used, 1)
                            if k == 1 and b < 3:
                                transposes(q + 1, 1)
                    if t < TT - 1:
                        last.then_inc(y_done, 1)
                    if b < 3 and t == 2:
                        transposes(q, 0)

            def first_units(b, u0, small_first=False):
                q = TT * b

                def part(j, t0, t1, final=False):
                    toks, s = slice(t0 * P, t1 * P), slot(u0 + j)
                    m = SMALL if small_first and j == 0 else P
                    if t0 == 0:
                        weights(u0 + j)
                    dst = bank[0:m, j, toks]
                    for k in range(KD):
                        w = slice(k * m, (k + 1) * m)
                        mm(dst, w_hi[:, s, w], u_hi[:, k, toks], start=k == 0, stop=False)
                        mm(dst, w_hi[:, s, w], u_lo[:, k, toks], start=False, stop=False)
                        last = mm(dst, w_lo[:, s, w], u_hi[:, k, toks], start=False, stop=k == KD - 1)
                    if final:
                        last.then_inc(unit_used, 1)

                pe.wait_ge(uT_lo, q + 2)
                part(0, 0, 2)
                part(1, 0, 2)
                transposes(q + 2, 2)
                part(2, 0, 2)
                transposes(q + 3, 3)
                part(3, 0, 2)
                pe.wait_ge(uT_lo, q + 4)
                for j in range(4):
                    part(j, 2, 4, True)

            def ffn(u0, layer, a0, b):
                first_units(b - 1, u0)
                with pe.Fori(1, KF // 2) as i:
                    for j in range(4):
                        if j % 2 == 0:
                            pe.wait_ge(hidden_ready, i * 2 + (layer * KF + j // 2 + 1))
                        weights(u0 + j, i, 4)
                        feature_product(u0 + j, bank[:, j, :]).then_inc(unit_used, 1)
                ud = u0 + 2 * KF

                def down(k, i=0, first=False):
                    weights(ud + k, i, 4)
                    pe.wait_ge(a_lo_ready, i * 4 + (a0 + k + 1))
                    for n, t in enumerate((0, 2, 3, 1)):
                        if first and t < 2:
                            pe.wait_ge(hidden_ready, PAIRS + layer * KF + KF - 1 + t)
                        last = token_product(ud + k, t, first, False)
                    last.then_inc(unit_used, 1)

                for k in range(4):
                    down(k, first=k == 0)
                with pe.Fori(0, 3) as i:
                    for j in range(4, 8):
                        down(j, i)
                down(16)
                down(17)
                last_units(b, ud + 18, a0 + 18)

            pe.wait_ge(consts, 1)
            transposes(0, 0)
            transposes(1, 1)
            ffn(U_FFN1, 0, A_FFN1, 1)

            first_units(1, U_MIX, small_first=True)
            pe.wait_ge(evac, 1)
            pe.wait_ge(w_al_in, 16)
            for j in range(2):
                mm(bank[:, 6 + j, :], w_al[ALR:ALR + RANK, j * P:(j + 1) * P], small[ALR:ALR + RANK, :],
                   start=True, stop=True).then_inc(z_ready, 1)
            bank_evac = {U_FQ + 3: 1, U_FV: 5, U_GV: 9}
            for s in range(4, INPUT):
                v = U_MIX + s
                weights(v)
                if v in bank_evac:
                    pe.wait_ge(evac, bank_evac[v])
                if v in (U_FQ + 1, U_FQ + 2):
                    pe.wait_ge(z_out, v - U_FQ)
                if v in plain:
                    last = feature_product(v, bank[:, feature_bank(v), :])
                else:
                    first, banks = (U_FV, FV_BANKS) if v < U_GV else (U_GV, GV_BANKS)
                    for kk in range(2):
                        k = 2 * (v - first) + kk
                        w = slice(kk * HALF, (kk + 1) * HALF)
                        for t in range(TT):
                            toks = slice(t * P, (t + 1) * P)
                            dst = bank[:, banks[t], :]
                            mm(dst, u_hi[:, k, toks], w_hi[:, slot(v), w], start=k == 0, stop=False)
                            mm(dst, u_hi[:, k, toks], w_lo[:, slot(v), w], start=False, stop=False)
                            last = mm(dst, u_lo[:, k, toks], w_hi[:, slot(v), w], start=False, stop=k == KD - 1)
                last.then_inc(unit_used, 1)

            pe.wait_ge(evac, 13)
            pe.wait_ge(c_ready, 1)
            read = {"kst": lambda n: (kst_copied, n + 1), "attn": lambda n: (attn_copied, 2 * n + 2),
                    "kv": lambda n: (state_ready, (NCH - 1) * (n // 2 + 1)), "o": lambda n: (on_ready, n + 1),
                    "ms": lambda n: (ms_out, n + 1)}
            for sl in range(SLOTS_B):
                if sl < NS:
                    hh, qb = steps[sl]
                    kend, rows, toks = (qb + 1) * P, slice(64 * (hh % 2), 64 * (hh % 2) + 64), slice(qb * P, (qb + 1) * P)
                    dst = bank[:, B_S[sl % 2], 0:kend]
                    if sl >= 2:
                        pe.wait_ge(exp_done, sl - 1)
                    mm(dst, arena[rows, T_Q + hh // 2, toks], arena[rows, T_K + hh // 2, 0:kend], start=True, stop=False)
                    crows = slice(rows.start, rows.start + 32 + FOX_H)
                    sel_h = head_sel[crows, hh, 0:1]
                    mm(dst, c_parts[crows, toks], sel_h.to_broadcast([32 + FOX_H, kend]), start=False, stop=False)
                    mm(dst, sel_h.to_broadcast([32 + FOX_H, P]), c_neg[crows, 0:kend], start=False, stop=False)
                    mm(dst[:, qb * P:kend], ident_r[:, :], causal[:, :], start=False, stop=True).then_inc(scores_ready, 1)
                if sl in FILL:
                    f, k_tiles = FILL[sl]
                    if k_tiles[0] == 0:
                        weights(U_GQ + f)
                        pe.wait_ge(evac, INPUT + f if f else 13)
                    last = feature_product(U_GQ + f, bank[:, B_FILL, :], k_tiles)
                    if k_tiles[-1] == KD - 1:
                        last.then_inc(unit_used, 1)
                for g in gla_slots.get(sl, ()):
                    kind, n = gla_steps[g]
                    if g == 0:
                        pe.wait_ge(evac, INPUT)
                        pe.wait_ge(a_dve, 7)
                    if g >= 2:
                        pk, pn = gla_steps[g - 2]
                        pe.wait_ge(*read[pk](pn))
                    dst = gbank(g)
                    if kind == "kst":
                        for t in (2 * n, 2 * n + 1):
                            for j in range(2):
                                c = (t % 2) * 2 * P + j * P
                                last = nc.tensor.transpose(dst[:, c:c + P], arena[:, T_KST + j, t * P:(t + 1) * P], ident[:, :])
                        last.then_inc(kst_ready, 1)
                    if kind == "attn":
                        rows = slice(64 * (n % 2), 64 * (n % 2) + 64)
                        for t in range(TT):
                            toks = slice(t * P, (t + 1) * P)
                            last = mm(dst[:, toks], arena[rows, T_GK + n // 2, toks], arena[rows, T_GQ + n // 2, toks],
                                      start=True, stop=True)
                        last.then_inc(attn_ready, 1)
                    if kind == "kv":
                        j, part_n = n // 2, n % 2
                        pe.wait_ge(kst_copied, 2)
                        for c in range(part_n, NCH - 1, 2):
                            rows = slice(CHUNK * part_n, CHUNK * part_n + CHUNK)
                            for e in range(2):
                                hh = 2 * j + e
                                last = mm(dst[64 * e:64 * e + 64, (c // 2) * P:(c // 2 + 1) * P],
                                          kst_tok[rows, c // 2, hh * GLA_DK:(hh + 1) * GLA_DK],
                                          arena[rows, T_GV + c // 2, hh * GLA_DV:(hh + 1) * GLA_DV], start=True, stop=True)
                        last.then_inc(kv_ready, 1)
                    if kind == "o":
                        pe.wait_ge(attn_masked, 2 * n + 2)
                        pe.wait_ge(state_ready, (NCH - 1) * (n // 2 + 1))
                        rows_k = slice(64 * (n % 2), 64 * (n % 2) + 64)
                        for t in range(TT):
                            mm(dst[:, t * P:(t + 1) * P], arena[:, T_GV + t, n * GLA_DV:(n + 1) * GLA_DV],
                               intra[:, n % 2, t, :], start=True, stop=False)
                            for c in (2 * t, 2 * t + 1):
                                if c:
                                    cols = slice(c * CHUNK, (c + 1) * CHUNK)
                                    last = mm(dst[:, cols], state[rows_k, c, :], arena[rows_k, T_GQ + n // 2, cols],
                                              start=False, stop=c % 2 == 1)
                        last.then_inc(o_ready, 1)
                    if kind == "ms":
                        pe.wait_ge(sq_ready, n + 1)
                        mm(dst, mean_g[:, :], msq[:, n, :], start=True, stop=True).then_inc(gms_ready, 1)
                if 2 <= sl < NS + 2:
                    s = sl - 2
                    pe.wait_ge(probs_ready, s + 1)
                    if s >= 2:
                        pe.wait_ge(pt_copied, s - 1)
                    for kb in range(steps[s][1] + 1):
                        cols = slice(kb * P, (kb + 1) * P)
                        last = nc.tensor.transpose(bank[:, B_PT[s % 2], cols], probs[steps[s][1]][:, cols], ident[:, :])
                    last.then_inc(pt_ready, 1)
                if 3 <= sl < NS + 3:
                    s = sl - 3
                    hh, qb = steps[s]
                    pair = hh // 2
                    pe.wait_ge(pt_copied, s + 1)
                    if s == 0:
                        pe.wait_ge(evac, 14)
                    elif s % 8 == 0:
                        pe.wait_ge(fox_lo, pair)
                    for kb in range(qb + 1):
                        last = mm(bank[64 * (hh % 2):64 * (hh % 2) + 64, B_OT, qb * P:(qb + 1) * P],
                                  arena[:, T_V + kb, hh * FOX_D:(hh + 1) * FOX_D], probsT[:, s % 2, kb * P:(kb + 1) * P],
                                  start=kb == 0, stop=kb == qb)
                    last.then_inc(pv_done, 1)

            pe.wait_ge(evac, 25)
            pe.wait_ge(pt_copied, NS)
            pe.wait_ge(on_ready, GLA_H)
            with pe.Fori(0, KD // 4) as i:
                for m in range(4):
                    b0, v = 4 * ((m + 1) % 2), U_GATE + 3 * m
                    pe.wait_ge(merged, i * 4 + (m + TILES - 1))
                    if m == 1:
                        pe.wait_ge(fox_lo, FOX_H // 2)
                    for j in range(2):
                        weights(v + j, i, 12)
                        feature_product(v + j, bank[:, b0 + j, :]).then_inc(unit_used, 1)
                    weights(v + 2, i, 12)
                    pe.wait_ge(fox_lo, FOX_H // 2)
                    feature_product(v + 2, bank[:, b0 + 2, :], range(4), of_hi, of_lo, 0, 3).then_inc(fox_used, 1)
                    pe.wait_ge(og_lo_ready, GLA_H)
                    feature_product(v + 2, bank[:, b0 + 3, :], range(4, 8), og_hi, og_lo, 4, 7).then_inc(unit_used, 1)

            for k in range(4):
                weights(U_OUT + k)
                pe.wait_ge(a_lo_ready, A_OUT + k + 1)
                for t in (2, 3, 0, 1):
                    if k == 0:
                        pe.wait_ge(merged, TILES + (KD - 1 if t >= 2 else KD))
                    last = token_product(U_OUT + k, t, k == 0, False)
                last.then_inc(unit_used, 1)
            last_units(2, U_OUT + 4, A_OUT + 4)
            ffn(U_FFN2, 1, A_FFN2, 3)

        @block.gpsimd
        def _(pool):
            G = nc.gpsimd
            G.dma_start(g_pre, gain(g1pre)).then_inc(g_pre_in, 16)
            G.dma_start(g_post, gain(g1post)).then_inc(g_post_in, 16)
            G.memset(half_neg[:, :], -0.5).then_inc(const_step, 1)
            G.memset(ident[:, :], 0.0).then_inc(const_step, 1)
            G.memset(arena[:, 0, 0:P], 0.0).then_inc(const_step, 1)
            sel = arena[0:CROWS, 1, 0:2 * FOX_H]
            G.memset(sel, 0.0).then_inc(const_step, 1)
            pool.wait_ge(const_step, 4)
            G.affine_select(out=ident[:, :], in_=ident[:, :], compare_op=ALU.not_equal, fill=1.0, base=0,
                            pattern=[[-1, P]], channel_multiplier=1).then_inc(const_step, 1)
            G.affine_select(out=arena[:, 0, 0:P], in_=arena[:, 0, 0:P], compare_op=ALU.is_ge, fill=MASKED, base=0,
                            pattern=[[-1, P]], channel_multiplier=1).then_inc(const_step, 1)
            selv = sel.rearrange("p (h o) -> p h o", o=2)
            for n in range(4):
                if n:
                    pool.wait_ge(const_step, 6 + n)
                G.affine_select(out=selv, in_=selv, compare_op=ALU.not_equal, fill=1.0, base=-32 * n,
                                pattern=[[-1, FOX_H], [0, 2]], channel_multiplier=1).then_inc(const_step, 1)

            def rsqrt(arrived, n, ms, ve, rstd, stepped, ready, eps):
                pool.wait_ge(arrived, n + 1)
                c = slice(n, n + 1)
                G.tensor_scalar(ve[:, c], ms[:, c], eps, None, ALU.add).then_inc(stepped, 1)
                pool.wait_ge(stepped, n + 1)
                G.tensor_tensor(rstd[:, c], ve[:, c], half_neg[:, :], ALU.pow).then_inc(ready, 1)

            def pre(n):
                rsqrt(pre_ms, n, ms_pre, ve_pre, rstd_pre, pre_ve, pre_rstd, EPS)

            def post(n, half):
                rsqrt(post_ms, n, ms_post, ve_post, rstd_post, post_ve, post_rstd, 4 * EPS if half else EPS)

            def between(b, half, u_next):
                for t in range(TT):
                    post(TT * b + t, half)
                    if t != 2:
                        if t == 3:
                            pre(TT * (b + 1) + 2)
                            u = u_next + 2
                            pool.wait_ge(hi_ready, u + 1)
                            pool.wait_ge(lo_ready, u)
                            G.tensor_tensor(w_lo[:, slot(u), :], raw[:, slot(u), :], w_hi[:, slot(u), :].bitcast(F32),
                                            ALU.subtract).then_inc(lo_ready, 1)
                        pre(TT * (b + 1) + t)

            for t in range(TT):
                pre(t)
            pool.wait_ge(normed_ready, TT)
            G.dma_start(g_pre, gain(gmpre)).then_inc(g_pre_in, 16)
            between(0, True, U_MIX)
            pool.wait_ge(c_ready, 1)
            G.memset(scr[:, 2048:3072], 0.0).then_inc(intra_zeroed, 1)
            for n in range(GLA_H):
                pool.wait_ge(attn_copied, 2 * n + 2)
                for c in range(2):
                    rows = slice(c * CHUNK, (c + 1) * CHUNK)
                    blk = intra[rows, n % 2, :, rows]
                    G.affine_select(out=blk, in_=blk, compare_op=ALU.is_ge, fill=0.0, base=0,
                                    pattern=[[0, TT], [1, CHUNK]], channel_multiplier=-1).then_inc(attn_masked, 1)
            pool.wait_ge(og_lo_ready, GLA_H)
            pool.wait_ge(pt_ready, NS)
            G.dma_start(g_pre, gain(g2pre)).then_inc(g_pre_in, 16)
            G.dma_start(g_post, gain(gmpost)).then_inc(g_post_in, 16)
            between(1, False, U_FFN2)
            pool.wait_ge(y_scaled, 2 * TT)
            G.dma_start(g_post, gain(g2post)).then_inc(g_post_in, 16)
            for t in range(TT):
                post(2 * TT + t, True)


_INS = ["x", "ffn1_pre_g", "ffn1_w_gate", "ffn1_w_up", "ffn1_w_down", "ffn1_post_g", "mix_pre_g", "w_in",
        "b_forget", "w_alpha_up", "b_alpha", "gla_norm_g", "w_branch_fox", "w_branch_gla", "w_out",
        "mix_post_g", "ffn2_pre_g", "ffn2_w_gate", "ffn2_w_up", "ffn2_w_down", "ffn2_post_g"]


def kernel(**inputs):
    import numpy as np
    import concourse.bacc as bacc
    from concourse.bass_utils import run_bass_kernel_spmd

    nc = bacc.Bacc("TRN2", target_bir_lowering=False, num_devices=1)
    arrays, args = {}, []
    for name in _INS:
        a = np.ascontiguousarray(inputs[name])[0]
        arrays[f"in_{name}"] = a
        args.append(nc.dram_tensor(f"in_{name}", a.shape, mybir.dt.from_np(a.dtype), kind="ExternalInput").ap())
    out = nc.dram_tensor("out", (N, D), F32, kind="ExternalOutput").ap()
    macaron_layer(nc, *args, out)
    r = run_bass_kernel_spmd(nc, [arrays], core_ids=[0])
    return np.asarray(r.results[0]["out"]).reshape(1, N, D)
```
